# Optimizing a Trainium2 kernel written in Bass

```python
import jax, jax.numpy as jnp
from jax import lax
import numpy as np

D_MODEL = 1024
BATCH = 1
SEQ = 1024
DEPTH = 2

GRID_W = 64
CTX_LEN = 256
EPS = 1e-6
NEG_INF = -1e30

N_MIXERS = 4
MIX_DELTANET = 0
MIX_POOL = 1
MIX_SWA = 2
MIX_CONV = 3
CTX_READING_MIXERS = (MIX_DELTANET, MIX_SWA)

DN_HEADS = 8
DN_HEAD_DIM = D_MODEL // DN_HEADS
DN_DIM = DN_HEADS * DN_HEAD_DIM
DN_CONV = 5
DN_CHUNK = 64

POOL_WINDOWS = (2, 4, 8, 16)
POOL_GROUP = D_MODEL // len(POOL_WINDOWS)

SWA_HEADS = 16
SWA_KV_HEADS = 4
SWA_HEAD_DIM = D_MODEL // SWA_HEADS
SWA_GROUP = SWA_HEADS // SWA_KV_HEADS
SWA_DIM = SWA_HEADS * SWA_HEAD_DIM
SWA_KV_DIM = SWA_KV_HEADS * SWA_HEAD_DIM
SWA_WINDOW = 128
SWA_BLOCK = 128
ROPE_BASE = 10000.0

CNV_WIDTH = 31

FFN_DIM = 2816
FFN_CONV = 3

kernel_name = 'hybrid_interleaved_dit_block'

def _layers_of(kind):
    return len(range(kind, DEPTH, N_MIXERS))

def rms_norm(x, w):
    xf = x.astype(jnp.float32)
    y = xf * lax.rsqrt(jnp.mean(xf * xf, axis=-1, keepdims=True) + EPS)
    return (y * w.astype(jnp.float32)).astype(x.dtype)

def layer_norm(x, w, b):
    xf = x.astype(jnp.float32)
    mu = jnp.mean(xf, axis=-1, keepdims=True)
    xc = xf - mu
    var = jnp.mean(xc * xc, axis=-1, keepdims=True)
    return (xc * lax.rsqrt(var + EPS) * w.astype(jnp.float32) + b.astype(jnp.float32)).astype(x.dtype)

def l2norm(x):
    return x * lax.rsqrt(jnp.sum(x * x, axis=-1, keepdims=True) + EPS)

def dw_conv(x, w):
    pad = w.shape[0] // 2
    return lax.conv_general_dilated(x, w.astype(x.dtype)[:, None, :], window_strides=(1,),
                                    padding=[(pad, pad)], dimension_numbers=('NWC', 'WIO', 'NWC'),
                                    feature_group_count=x.shape[-1])

def _ada(cond, w, b):
    m = jax.nn.silu(cond) @ w + b
    return jnp.split(m, 6, axis=-1)

def axial_rope_tables(n_rows, head_dim):
    n_freq = head_dim // 4
    inv_freq = ROPE_BASE ** (-jnp.arange(n_freq, dtype=jnp.float32) / n_freq)
    rows = jnp.repeat(jnp.arange(n_rows, dtype=jnp.float32), GRID_W)
    cols = jnp.tile(jnp.arange(GRID_W, dtype=jnp.float32), n_rows)
    ang_r = rows[:, None] * inv_freq
    ang_c = cols[:, None] * inv_freq
    ang = jnp.concatenate([ang_r, ang_r, ang_c, ang_c], axis=-1)
    return jnp.cos(ang), jnp.sin(ang)

def apply_axial_rope(x, cos, sin):
    xf = x.astype(jnp.float32)
    x1, x2, x3, x4 = jnp.split(xf, 4, axis=-1)
    rot = jnp.concatenate([-x2, x1, -x4, x3], axis=-1)
    shp = (1, cos.shape[0]) + (1,) * (x.ndim - 3) + (cos.shape[-1],)
    return (xf * cos.reshape(shp) + rot * sin.reshape(shp)).astype(x.dtype)

def gated_delta_chunked(q, k, v, beta, g, s0):
    B, H, T, dk = q.shape
    dv = v.shape[-1]
    C = DN_CHUNK
    N = T // C
    q = q.reshape(B, H, N, C, dk) * (dk ** -0.5)
    k = k.reshape(B, H, N, C, dk)
    v = v.reshape(B, H, N, C, dv)
    beta = beta.reshape(B, H, N, C)
    gc = jnp.cumsum(g.reshape(B, H, N, C), axis=-1)
    idx = jnp.arange(C)
    lower = idx[:, None] >= idx[None, :]
    strict = idx[:, None] > idx[None, :]
    diff = gc[..., :, None] - gc[..., None, :]
    decay_mat = jnp.where(lower, jnp.exp(jnp.where(lower, diff, 0.0)), 0.0)
    kk = jnp.einsum('bhncd,bhnmd->bhncm', k, k)
    t_mat = jnp.where(strict, beta[..., None] * kk * decay_mat, 0.0) + jnp.eye(C, dtype=jnp.float32)
    rhs = jnp.concatenate([v * beta[..., None], k * (beta * jnp.exp(gc))[..., None]], axis=-1)
    sol = lax.linalg.triangular_solve(t_mat, rhs, left_side=True, lower=True, unit_diagonal=True)
    u, w = sol[..., :dv], sol[..., dv:]
    qk = jnp.where(lower, jnp.einsum('bhncd,bhnmd->bhncm', q, k) * decay_mat, 0.0)
    g_last = gc[..., -1]
    k_dec = k * jnp.exp(g_last[..., None] - gc)[..., None]
    q_dec = q * jnp.exp(gc)[..., None]

    def step(S, xs):
        q_c, qk_c, u_c, w_c, k_c, gl_c = xs
        v_new = u_c - jnp.einsum('bhcd,bhde->bhce', w_c, S)
        o = jnp.einsum('bhcd,bhde->bhce', q_c, S) + jnp.einsum('bhcm,bhme->bhce', qk_c, v_new)
        S = S * jnp.exp(gl_c)[..., None, None] + jnp.einsum('bhcd,bhce->bhde', k_c, v_new)
        return S, o

    xs = tuple(jnp.moveaxis(a, 2, 0) for a in (q_dec, qk, u, w, k_dec, g_last))
    s_final, o = lax.scan(step, s0, xs)
    o = jnp.moveaxis(o, 0, 2).reshape(B, H, T, dv)
    return o, s_final

def deltanet_mixer(h_lat, h_ctx, w_in, conv_w, a_log, dt_bias, norm_w, w_out, ctx_out):
    def project(h):
        b_, t_, _ = h.shape
        p = h @ w_in
        qkv = jax.nn.silu(dw_conv(p[..., :3 * DN_DIM], conv_w))
        z = p[..., 3 * DN_DIM:4 * DN_DIM]
        gates = p[..., 4 * DN_DIM:].astype(jnp.float32).reshape(b_, t_, 4, DN_HEADS).transpose(2, 0, 3, 1)
        heads = qkv.astype(jnp.float32).reshape(b_, t_, 3, DN_HEADS, DN_HEAD_DIM).transpose(2, 0, 3, 1, 4)
        q, k, v = l2norm(heads[0]), l2norm(heads[1]), heads[2]
        beta = jax.nn.sigmoid(gates[:2])
        g = -jnp.exp(a_log.astype(jnp.float32))[:, None, :, None] * jax.nn.softplus(
            gates[2:] + dt_bias.astype(jnp.float32)[:, None, :, None])
        return q, k, v, z, beta, g

    def scan_dir(q, k, v, beta, g, s0, backward):
        if backward:
            fl = lambda a: jnp.flip(a, axis=2)
            o, s = gated_delta_chunked(fl(q), fl(k), fl(v), fl(beta), fl(g), s0)
            return fl(o), s
        return gated_delta_chunked(q, k, v, beta, g, s0)

    def readout(o, z):
        b_, _, t_, _ = o.shape
        o = rms_norm(o.transpose(0, 2, 1, 3), norm_w)
        o = o * jax.nn.silu(z.astype(jnp.float32).reshape(b_, t_, DN_HEADS, DN_HEAD_DIM))
        return o.reshape(b_, t_, DN_DIM).astype(z.dtype) @ w_out

    qc, kc, vc, zc, bc, gc = project(h_ctx)
    ql, kl, vl, zl, bl, gl = project(h_lat)
    s0 = jnp.zeros((h_ctx.shape[0], DN_HEADS, DN_HEAD_DIM, DN_HEAD_DIM), jnp.float32)
    oc_f, sc_f = scan_dir(qc, kc, vc, bc[0], gc[0], s0, False)
    oc_b, sc_b = scan_dir(qc, kc, vc, bc[1], gc[1], s0, True)
    ol_f, _ = scan_dir(ql, kl, vl, bl[0], gl[0], sc_f, False)
    ol_b, _ = scan_dir(ql, kl, vl, bl[1], gl[1], sc_b, True)
    y_lat = readout(ol_f + ol_b, zl)
    y_ctx = readout(oc_f + oc_b, zc) if ctx_out else None
    return y_lat, y_ctx

def pool_mixer(h, w_grp, scale):
    T = h.shape[1]
    hf = h.astype(jnp.float32)
    csum = jnp.pad(jnp.cumsum(hf, axis=1), ((0, 0), (1, 0), (0, 0)))
    t = jnp.arange(T)
    outs = []
    for gi, win in enumerate(POOL_WINDOWS):
        sl = slice(gi * POOL_GROUP, (gi + 1) * POOL_GROUP)
        cs = csum[..., sl]
        lo = jnp.clip(t - win // 2, 0, T)
        hi = jnp.clip(t + win - win // 2, 0, T)
        mean = (cs[:, hi] - cs[:, lo]) / (hi - lo).astype(jnp.float32)[None, :, None]
        d = (mean - hf[..., sl]).astype(h.dtype)
        outs.append(d @ w_grp[gi])
    return jnp.concatenate(outs, axis=-1) * scale

def _sink_softmax(sink_logit, *parts):
    lead = parts[0].shape[:-1]
    s = jnp.broadcast_to(sink_logit, lead + (1,))
    return jax.nn.softmax(jnp.concatenate((s,) + parts, axis=-1), axis=-1)

def swa_mixer(h_lat, h_ctx, w_qkv, q_norm_w, k_norm_w, sink, w_out, cos, sin, ctx_out):
    scale = SWA_HEAD_DIM ** -0.5

    def project(h):
        b_, t_, _ = h.shape
        p = h @ w_qkv
        q = p[..., :SWA_DIM].reshape(b_, t_, SWA_KV_HEADS, SWA_GROUP, SWA_HEAD_DIM)
        k = p[..., SWA_DIM:SWA_DIM + SWA_KV_DIM].reshape(b_, t_, SWA_KV_HEADS, SWA_HEAD_DIM)
        v = p[..., SWA_DIM + SWA_KV_DIM:].reshape(b_, t_, SWA_KV_HEADS, SWA_HEAD_DIM)
        return rms_norm(q, q_norm_w), rms_norm(k, k_norm_w), v

    B, T, _ = h_lat.shape
    q_l, k_l, v_l = project(h_lat)
    q_l = apply_axial_rope(q_l, cos, sin)
    k_l = apply_axial_rope(k_l, cos, sin)
    q_c, k_c, v_c = project(h_ctx)
    sink_logit = sink.astype(jnp.float32).reshape(SWA_KV_HEADS, SWA_GROUP)[None, :, :, None, None]

    span = SWA_BLOCK + 2 * SWA_WINDOW
    kp = jnp.pad(k_l, ((0, 0), (SWA_WINDOW, SWA_WINDOW), (0, 0), (0, 0)))
    vp = jnp.pad(v_l, ((0, 0), (SWA_WINDOW, SWA_WINDOW), (0, 0), (0, 0)))
    rel = jnp.arange(span)[None, :] - SWA_WINDOW - jnp.arange(SWA_BLOCK)[:, None]
    band = jnp.abs(rel) <= SWA_WINDOW

    def block(b):
        start = b * SWA_BLOCK
        qb = lax.dynamic_slice_in_dim(q_l, start, SWA_BLOCK, axis=1)
        kb = lax.dynamic_slice_in_dim(kp, start, span, axis=1)
        vb = lax.dynamic_slice_in_dim(vp, start, span, axis=1)
        kpos = start - SWA_WINDOW + jnp.arange(span)
        valid = band & ((kpos >= 0) & (kpos < T))[None, :]
        s_loc = jnp.einsum('bqhgd,bkhd->bhgqk', qb, kb, preferred_element_type=jnp.float32) * scale
        s_loc = jnp.where(valid, s_loc, NEG_INF)
        s_ctx = jnp.einsum('bqhgd,bkhd->bhgqk', qb, k_c, preferred_element_type=jnp.float32) * scale
        p = _sink_softmax(sink_logit, s_loc, s_ctx)
        p_loc = p[..., 1:1 + span].astype(vb.dtype)
        p_ctx = p[..., 1 + span:].astype(v_c.dtype)
        return jnp.einsum('bhgqk,bkhd->bqhgd', p_loc, vb) + jnp.einsum('bhgqk,bkhd->bqhgd', p_ctx, v_c)

    o_l = lax.map(block, jnp.arange(T // SWA_BLOCK))
    y_lat = jnp.moveaxis(o_l, 0, 1).reshape(B, T, SWA_DIM) @ w_out
    y_ctx = None
    if ctx_out:
        L = h_ctx.shape[1]
        s_cc = jnp.einsum('bqhgd,bkhd->bhgqk', q_c, k_c, preferred_element_type=jnp.float32) * scale
        p_cc = _sink_softmax(sink_logit, s_cc)[..., 1:].astype(v_c.dtype)
        y_ctx = jnp.einsum('bhgqk,bkhd->bqhgd', p_cc, v_c).reshape(h_ctx.shape[0], L, SWA_DIM) @ w_out
    return y_lat, y_ctx

def conv_module(h, w_pw1, dw, ln_w, ln_b, w_pw2):
    a = h @ w_pw1
    u = a[..., :D_MODEL] * jax.nn.sigmoid(a[..., D_MODEL:])
    u = jax.nn.silu(layer_norm(dw_conv(u, dw), ln_w, ln_b))
    return u @ w_pw2

def conv_ffn(h, w_gate, w_up, conv_w, conv_b, w_down):
    g = dw_conv(h @ w_gate, conv_w) + conv_b
    return (jax.nn.silu(g) * (h @ w_up)) @ w_down

def setup_inputs(seed: int = 0) -> dict:
    key = jax.random.key(seed)
    ks = iter(jax.random.split(key, 48))
    D = D_MODEL
    nrm = lambda shape, s: jax.random.normal(next(ks), shape, jnp.float32) * s
    n_dn, n_pool, n_swa, n_cnv = (_layers_of(MIX_DELTANET), _layers_of(MIX_POOL),
                                  _layers_of(MIX_SWA), _layers_of(MIX_CONV))
    dn_a_log = jnp.log(jax.random.uniform(next(ks), (n_dn, 2, DN_HEADS), jnp.float32, 1.0, 16.0))
    dt = jnp.exp(jax.random.uniform(next(ks), (n_dn, 2, DN_HEADS), jnp.float32,
                                    float(np.log(1e-3)), float(np.log(1e-1))))
    dn_dt_bias = dt + jnp.log(-jnp.expm1(-dt))
    return {
        'x': nrm((BATCH, SEQ, D), 1.0),
        'c': nrm((BATCH, D), 1.0),
        'ctx': nrm((BATCH, CTX_LEN, D), 1.0),
        'c_ctx': nrm((D,), 1.0),
        'ada_w': nrm((DEPTH, D, 6 * D), 0.5 * D ** -0.5),
        'ada_b': nrm((DEPTH, 6 * D), 0.01),
        'norm_mix_w': 1.0 + nrm((DEPTH, D), 0.02),
        'norm_ffn_w': 1.0 + nrm((DEPTH, D), 0.02),
        'dn_w_in': nrm((n_dn, D, 4 * DN_DIM + 4 * DN_HEADS), D ** -0.5),
        'dn_conv': nrm((n_dn, DN_CONV, 3 * DN_DIM), DN_CONV ** -0.5),
        'dn_a_log': dn_a_log,
        'dn_dt_bias': dn_dt_bias,
        'dn_norm_w': 1.0 + nrm((n_dn, DN_HEAD_DIM), 0.02),
        'dn_w_out': nrm((n_dn, DN_DIM, D), DN_DIM ** -0.5),
        'pool_w_grp': nrm((n_pool, len(POOL_WINDOWS), POOL_GROUP, POOL_GROUP), POOL_GROUP ** -0.5),
        'pool_scale': 1.0 + nrm((n_pool, D), 0.1),
        'swa_w_qkv': nrm((n_swa, D, SWA_DIM + 2 * SWA_KV_DIM), D ** -0.5),
        'swa_q_norm': 1.0 + nrm((n_swa, SWA_HEAD_DIM), 0.02),
        'swa_k_norm': 1.0 + nrm((n_swa, SWA_HEAD_DIM), 0.02),
        'swa_sink': nrm((n_swa, SWA_HEADS), 1.0),
        'swa_w_out': nrm((n_swa, SWA_DIM, D), SWA_DIM ** -0.5),
        'cnv_w_pw1': nrm((n_cnv, D, 2 * D), D ** -0.5),
        'cnv_dw': nrm((n_cnv, CNV_WIDTH, D), CNV_WIDTH ** -0.5),
        'cnv_ln_w': 1.0 + nrm((n_cnv, D), 0.02),
        'cnv_ln_b': nrm((n_cnv, D), 0.01),
        'cnv_w_pw2': nrm((n_cnv, D, D), D ** -0.5),
        'ffn_w_gate': nrm((DEPTH, D, FFN_DIM), D ** -0.5),
        'ffn_w_up': nrm((DEPTH, D, FFN_DIM), D ** -0.5),
        'ffn_conv': nrm((DEPTH, FFN_CONV, FFN_DIM), FFN_CONV ** -0.5),
        'ffn_conv_b': nrm((DEPTH, FFN_DIM), 0.01),
        'ffn_w_down': nrm((DEPTH, FFN_DIM, D), FFN_DIM ** -0.5),
    }

def reference(x, c, ctx, c_ctx, ada_w, ada_b, norm_mix_w, norm_ffn_w,
              dn_w_in, dn_conv, dn_a_log, dn_dt_bias, dn_norm_w, dn_w_out,
              pool_w_grp, pool_scale,
              swa_w_qkv, swa_q_norm, swa_k_norm, swa_sink, swa_w_out,
              cnv_w_pw1, cnv_dw, cnv_ln_w, cnv_ln_b, cnv_w_pw2,
              ffn_w_gate, ffn_w_up, ffn_conv, ffn_conv_b, ffn_w_down):
    h, hc = x, ctx
    n_rows = x.shape[1] // GRID_W
    cos, sin = axial_rope_tables(n_rows, SWA_HEAD_DIM)
    for i in range(DEPTH):
        kind, slot = i % N_MIXERS, i // N_MIXERS
        keep_ctx = any((j % N_MIXERS) in CTX_READING_MIXERS for j in range(i + 1, DEPTH))
        need_ctx_in = keep_ctx or (kind in CTX_READING_MIXERS)
        sh1, sc1, gt1, sh2, sc2, gt2 = [m[:, None, :] for m in _ada(c, ada_w[i], ada_b[i])]
        hin = rms_norm(h, norm_mix_w[i]) * (1.0 + sc1) + sh1
        hcin = None
        if need_ctx_in:
            csh1, csc1, cgt1, csh2, csc2, cgt2 = _ada(c_ctx, ada_w[i], ada_b[i])
            hcin = rms_norm(hc, norm_mix_w[i]) * (1.0 + csc1) + csh1
        if kind == MIX_DELTANET:
            y, yc = deltanet_mixer(hin, hcin, dn_w_in[slot], dn_conv[slot], dn_a_log[slot], dn_dt_bias[slot],
                                   dn_norm_w[slot], dn_w_out[slot], keep_ctx)
        elif kind == MIX_POOL:
            y = pool_mixer(hin, pool_w_grp[slot], pool_scale[slot])
            yc = pool_mixer(hcin, pool_w_grp[slot], pool_scale[slot]) if keep_ctx else None
        elif kind == MIX_SWA:
            y, yc = swa_mixer(hin, hcin, swa_w_qkv[slot], swa_q_norm[slot], swa_k_norm[slot], swa_sink[slot],
                              swa_w_out[slot], cos, sin, keep_ctx)
        else:
            y = conv_module(hin, cnv_w_pw1[slot], cnv_dw[slot], cnv_ln_w[slot], cnv_ln_b[slot], cnv_w_pw2[slot])
            yc = (conv_module(hcin, cnv_w_pw1[slot], cnv_dw[slot], cnv_ln_w[slot], cnv_ln_b[slot], cnv_w_pw2[slot])
                  if keep_ctx else None)
        h = h + gt1 * y
        h = h + gt2 * conv_ffn(rms_norm(h, norm_ffn_w[i]) * (1.0 + sc2) + sh2,
                               ffn_w_gate[i], ffn_w_up[i], ffn_conv[i], ffn_conv_b[i], ffn_w_down[i])
        if keep_ctx:
            hc = hc + cgt1 * yc
            hc = hc + cgt2 * conv_ffn(rms_norm(hc, norm_ffn_w[i]) * (1.0 + csc2) + csh2,
                                      ffn_w_gate[i], ffn_w_up[i], ffn_conv[i], ffn_conv_b[i], ffn_w_down[i])
    return h


_drawn_inputs = setup_inputs


def setup_inputs(seed=0):
    import zlib

    import numpy as np

    out = dict(_drawn_inputs(seed))
    spreads = {}
    factors = {'ctx': 3.979,
     'c_ctx': 6.548,
     'ada_b': 3.481,
     'norm_mix_w': 7.776,
     'norm_ffn_w': 6.976,
     'dn_norm_w': 8.0,
     'ffn_conv_b': 45.555,
     'pool_scale': 4.487}
    for name, (base, spread) in spreads.items():
        noise = np.random.default_rng([zlib.crc32(name.encode()), seed]).standard_normal(out[name].shape)
        drawn = base * np.exp(spread * noise) if base else spread * noise
        out[name] = __import__('jax').numpy.asarray(drawn.astype(out[name].dtype))
    for name, factor in factors.items():
        out[name] = (out[name] * factor).astype(out[name].dtype)
    return out
```

```python
import concourse.bass as bass
import concourse.mybir as mybir
import numpy as np
from concourse.alu_op_type import AluOpType as ALU
from contextlib import ExitStack

F32 = mybir.dt.float32
F32R = mybir.dt.float32r
ACT = mybir.ActivationFunctionType

P = 128
D = 1024
KT = D // P
LAT = 1024
CTX = 256
TOK = LAT + CTX
HALF = 512
HEADS = 8
DK = D // HEADS
TAPS = 5
FFN = 2816
FT = FFN // P
FTAPS = 3
EPS = 1e-6
POOL_WINDOWS = (2, 4, 8, 16)
EDGE = max(POOL_WINDOWS) // 2
CHUNK = 128
NCHUNK = TOK // CHUNK
NCTX = CTX // CHUNK
NLAT = LAT // CHUNK
HG = 2
GH = HEADS // HG
LEVELS = (2, 4, 8, 16, 32, 64)
NL = len(LEVELS)
CKINDS = 6
UNIT = KT * P

_at = 0


def _cols(n):
    global _at
    _at += n
    return _at - n


C_COND = _cols(2 * KT)
C_ADAB = _cols(2 * 48)
C_NMIX = _cols(2 * KT)
C_NFFN = _cols(2 * KT)
C_CONV = _cols(3 * KT * TAPS)
C_DNW = _cols(1)
C_FCONV = _cols(2 * FT * FTAPS)
C_FBIAS = _cols(2 * FT)
C_PSCALE = _cols(KT)
C_ALOG = _cols(16)
C_DT = _cols(16)
C_EDGE = _cols(4 * 2 * EDGE)
C_EPS = _cols(1)
N_IN = _at
C_MODS = _cols(2 * 96)
C_SILU = _cols(2 * KT)
C_A = _cols(5 * KT)
C_PG = _cols(KT)
N_SMALL = _at
N_COL = NCHUNK * 2 * HG * CKINDS * GH

K_ID, K_ONES, K_TRIF, K_TRIB = 0, 1, 2, 3
K_QKF, K_QKB, K_NF, K_NB = 4, 5, 6, 7
K_LF = 8
K_LB = K_LF + NL + 1
N_CONST = K_LB + NL + 1

U_GATE, U_K, U_Q, U_V, U_Z, U_OUT = 0, 1, 9, 17, 25, 33
U_GU = (41, 41 + 2 * FT + 2 * FT + 2)
U_DN = (U_GU[0] + 2 * FT, U_GU[1] + 2 * FT)
U_POOL = U_DN[0] + 2 * FT
W_POOL = U_DN[0] + FT
W_GU = (U_GU[0], W_POOL + 2)
W_DN = (U_DN[0], W_GU[1] + 2 * FT)

BASE = 16512
KB = 1024
O_WRAW, O_WH, O_WL = 0, 8 * KB, 16 * KB
O_SMALL = 24 * KB
O_COL = O_SMALL + 4 * KB
O_A = 32 * KB


def constants():
    i = np.arange(P)
    r, c = i[:, None], i[None, :]
    m = np.zeros((N_CONST, P, P), np.float32)
    m[K_ID] = r == c
    m[K_ONES] = 1
    m[K_TRIF] = r <= c
    m[K_TRIB] = r >= c
    m[K_QKF] = c >= r
    m[K_QKB] = c <= r
    m[K_NF] = r > c
    m[K_NB] = r < c
    for n, s in enumerate((1,) + LEVELS):
        low = (r // (2 * s) == c // (2 * s)) & (r // s > c // s)
        m[K_LF + n] = (r == c) * 1.0 - low
        m[K_LB + n] = m[K_LF + n].T
    return np.ascontiguousarray(m.transpose(1, 0, 2)).reshape(P, N_CONST * P)


class Unit:

    def __init__(self, base, trip=None):
        self.base, self.trip, self.par = base, trip, base % 2

    def n(self, off=0):
        v = self.base + off
        return v if self.trip is None else self.trip * 2 + v

    def half(self, off=0):
        v = (self.base + off) // 2
        return v if self.trip is None else self.trip + v

    def plus(self, k):
        return Unit(self.base + k, self.trip)


class Chain:

    def __init__(self, eng, sem):
        self.eng, self.sem, self.n, self.trip, self.per = eng, sem, 0, None, 0

    def __call__(self, ins):
        ins.then_inc(self.sem, 1)
        self.n += 1
        v = self.n if self.trip is None else self.trip * self.per + self.n
        self.eng.wait_ge(self.sem, v)
        return ins

    def enter(self, trip, per, first=0):
        self.trip, self.per, self.n0 = trip, per, self.n
        self.n -= first * per

    def leave(self, trips, first=0):
        assert self.n + first * self.per == self.n0 + self.per, (self.n + first * self.per - self.n0, self.per)
        self.n, self.trip = self.n0 + trips * self.per, None


def need(eng, sem, value):
    if not isinstance(value, int) or value > 0:
        eng.wait_ge(sem, value)


def build(nc, xT, ctxT, small_in, const_in, ada_w, w_units, outT, kd, qd, vd, zd, hd):
    es = ExitStack()
    sems = {}

    def sem(name):
        if name not in sems:
            sems[name] = es.enter_context(nc.semaphore(name))
        return sems[name]

    def sb(name, cols, at, dt=F32, parts=P):
        assert BASE + at + 4 * cols <= 229368, (name, at, cols)
        return nc.alloc_sbuf_tensor_at(name, [parts, cols], dt, offset=BASE + at)

    with es:
        wraw = [sb(f"wraw{i}", UNIT, O_WRAW + 4 * KB * i) for i in range(2)]
        wh = [sb(f"wh{i}", UNIT, O_WH + 4 * KB * i, F32R) for i in range(2)]
        wl = [sb(f"wl{i}", UNIT, O_WL + 4 * KB * i, F32R) for i in range(2)]
        small = sb("small", N_SMALL, O_SMALL)
        col = sb("col", N_COL, O_COL)
        colv = col[:, :].rearrange("p (n d g k h) -> p n d g k h", n=NCHUNK, d=2, g=HG, k=CKINDS)
        hT = sb("hT", KT * LAT, O_A)
        hTv = hT[:, :].rearrange("p (k t) -> p k t", k=KT)
        fixed = sb("fixed", 2 * P, O_A + 173 * KB)
        ident, ones = fixed[:, 0:P], fixed[:, P:2 * P]
        ctxs = sb("ctxs", KT * CTX, O_A + 128 * KB)
        ctxv = ctxs[:, :].rearrange("p (k t) -> p k t", k=KT)
        EARLY = 3 * D
        adae = [sb(f"adae{i}", 2 * EARLY, O_A + (32 + 24 * i) * KB) for i in range(KT // 2)]
        mrow = sb("mrow", EARLY, O_A + 136 * KB, parts=2)
        acc0 = sb("acc0", EARLY, O_A + 128 * KB)
        adal = [sb(f"adal{i}", EARLY, O_A + (140 + 12 * i) * KB) for i in range(2)]
        PIECE = 1536
        PIECES = 6 * D // PIECE
        ROWS0 = 5
        acc1 = sb("acc1", 6 * D, O_A + 128 * KB)
        adap = [sb(f"adap{i}", PIECE, O_A + (152 + 6 * i) * KB) for i in range(2)]
        pxh = sb("pxh", KT * TOK, O_A + 32 * KB, F32R)
        pxl = sb("pxl", KT * TOK, O_A + 72 * KB, F32R)
        PADW = 2 + LAT + 2 + CTX + 2
        CONVW = LAT + 2 + CTX
        T0 = O_A + 112 * KB
        TS = 5184
        pad = [sb(f"pad{i}", PADW, T0 + TS * i) for i in range(2)]
        acc = [sb(f"acc{i}", CONVW, T0 + TS * (2 + i)) for i in range(2)]
        sl = [sb(f"sl{i}", CONVW, T0 + TS * (4 + i)) for i in range(2)]
        sq = [sb(f"sq{i}", CONVW, T0 + TS * (6 + i)) for i in range(2)]
        rs = sb("rs", CONVW, T0 + TS * 8)
        ob = [sb(f"ob{i}", CONVW, T0 + TS * (9 + i)) for i in range(2)]
        grow = sb("grow", TOK, T0 + TS * 11, parts=32)
        oT = sb("oT", HEADS * LAT, O_A + 32 * KB)
        oTv = oT[:, :].rearrange("p (h t) -> p h t", h=HEADS)
        const = sb("const", N_CONST * P, O_A + 64 * KB)
        cv = const[:, :].rearrange("p (n c) -> p n c", n=N_CONST)
        at = O_A + 64 * KB + N_CONST * P * 4
        BW = GH * P
        kq = {}
        for nm in "KQV":
            for par in range(2):
                for d in range(2):
                    kq[nm, par, d] = sb(f"in{nm}{par}{d}", BW, at)
                    at += 2 * KB
        S = {}
        for g in range(HG):
            for d in range(2):
                S[g, d] = sb(f"S{g}{d}", BW, at)
                at += 2 * KB
        tile = {}
        for nm in ("X", "XT", "TT", "TN", "Z", "Kbe", "Kdec", "Vb", "G", "GU", "GL", "qkT", "QdT", "WTn", "VN", "Sg"):
            for d in range(2):
                tile[nm, d] = sb(f"{nm}{d}", BW, at)
                at += 2 * KB
        assert at + 512 <= O_A + 173 * KB
        stage = [sb(f"stage{i}", 2 * CKINDS * GH, at + 256 * i) for i in range(2)]
        at += 512
        GN = NCHUNK * 32
        ga = [sb(f"ga{i}", GN, O_A + 120 * KB + 2 * KB * i) for i in range(6)]
        yh = sb("yh", HEADS * LAT, O_A + 64 * KB, F32R)
        yl = sb("yl", HEADS * LAT, O_A + 96 * KB, F32R)
        R0 = O_A + 128 * KB
        zt = [sb(f"zt{i}", LAT, R0 + 4 * KB * i) for i in range(2)]
        rsq = [sb(f"rsq{i}", LAT, R0 + (8 + 4 * i) * KB) for i in range(2)]
        rrs = [sb(f"rrs{i}", LAT, R0 + (16 + 4 * i) * KB) for i in range(2)]
        rt = [sb(f"rt{i}", LAT, R0 + (24 + 4 * i) * KB) for i in range(2)]
        rsq2 = sb("rscaled", LAT, R0 + 32 * KB)
        hid = sb("hid", FT * LAT, O_A)
        hidv = hid[:, :].rearrange("p (k t) -> p k t", k=FT)
        xh = sb("xh", KT * LAT, O_A + 88 * KB, F32R)
        xl = sb("xl", KT * LAT, O_A + 120 * KB, F32R)
        F0 = O_A + 152 * KB
        fpad = sb("fpad", LAT + 2, F0)
        facc = sb("facc", LAT, F0 + 4 * KB + 64)
        fsl = sb("fsl", LAT, F0 + 8 * KB + 64)
        h2 = sb("h2", KT * LAT, O_A + 88 * KB)
        h2v = h2[:, :].rearrange("p (k t) -> p k t", k=KT)
        dxh = [sb(f"dxh{i}", HALF, O_A + 120 * KB + 2 * KB * i, F32R) for i in range(2)]
        dxl = [sb(f"dxl{i}", HALF, O_A + 124 * KB + 2 * KB * i, F32R) for i in range(2)]
        nsq = [sb(f"nsq{i}", LAT, O_A + (152 + 4 * i) * KB) for i in range(2)]
        nrs = sb("nrs", LAT, O_A + 160 * KB)
        nt = [sb(f"nt{i}", LAT, O_A + (164 + 4 * i) * KB) for i in range(2)]
        h3 = sb("h3", KT * LAT, O_A + 32 * KB)
        h3v = h3[:, :].rearrange("p (k t) -> p k t", k=KT)
        PW = LAT + 2 * EDGE
        hin = sb("hin", KT * PW, O_A + 32 * KB)
        hinv = hin[:, :].rearrange("p (k t) -> p k t", k=KT)
        plh = sb("plh", KT * LAT, O_A, F32R)
        pll = sb("pll", KT * LAT, O_A + 120 * KB, F32R)
        pt = [sb(f"pt{i}", PW, O_A + 66 * KB + TS * i) for i in range(2)]
        pd = [sb(f"pd{i}", LAT, O_A + 66 * KB + TS * (2 + i)) for i in range(2)]
        assert 66 * KB + TS * 4 <= 88 * KB

        ps = es.enter_context(nc.psum_tensor("ps", [P, 8 * HALF], F32))
        bank = lambda b, n=1: ps[:, b * HALF:(b + n) * HALF]

        phase_end = sem("phase_end")
        w_loaded = [sem(f"w_loaded{i}") for i in range(2)]
        w_hi, w_lo, w_used = sem("w_hi"), sem("w_lo"), sem("w_used")
        sc = lambda c, n=1: small[:, c:c + n]
        mod = lambda layer, which, k, who: small[:, C_MODS + 96 * layer + 2 * (8 * which + k) + who:
                                                 C_MODS + 96 * layer + 2 * (8 * which + k) + who + 1]

        block = es.enter_context(nc.Block())

        def meet(eng, n):
            eng.drain().then_inc(phase_end, 1)
            eng.wait_ge(phase_end, 4 * n)

        start_loaded = sem("start_loaded")
        mods_done = sem("mods_done")

        def apart(act):
            act.wait_ge(start_loaded, 16)

        def load_unit(sp, u, where=None):
            need(sp, w_lo, u.n(-1))
            sp.dma_start(wraw[u.par][:, :], w_units[u.n() if where is None else where, :, :]).then_inc(w_loaded[u.par], 16)

        def cut_hi(act, u):
            act.wait_ge(w_loaded[u.par], 16 * (u.half() + 1))
            need(act, w_used, u.n(-1))
            act.activation(wh[u.par][:, :], wraw[u.par][:, :], ACT.Copy).then_inc(w_hi, 1)

        def cut_lo(dve, u):
            dve.wait_ge(w_hi, u.n(1))
            dve.tensor_tensor(wl[u.par][:, :], wraw[u.par][:, :], wh[u.par][:, :].bitcast(F32),
                              ALU.subtract).then_inc(w_lo, 1)

        def product(pe, u, outs, kt=KT, first=True, last=True):
            for k in range(kt):
                w = slice(k * P, (k + 1) * P)
                for n, (wt, lo) in enumerate(((wh, 0), (wh, 1), (wl, 0))):
                    for out, hi_of, lo_of in outs:
                        mm = pe.matmul(out, wt[u.par][:, w], (lo_of if lo else hi_of)(k),
                                       start=first and k == 0 and n == 0, stop=last and k == kt - 1 and n == 2)
            return mm

        norms = ("mix0", "ctx0", "ffn0", "mix1", "ffn1")
        NT = {"mix0": LAT, "ctx0": CTX, "ffn0": LAT, "mix1": LAT, "ffn1": LAT}

        def norm_src(name, k):
            if name == "ctx0":
                return ctxv[:, k, :]
            return {"mix0": hTv, "ffn0": hTv, "mix1": h2v, "ffn1": h3v}[name][:, k, :]

        def norm_dst(name, k, lo):
            if name == "mix0":
                return (pxl if lo else pxh)[:, :].rearrange("p (k t) -> p k t", k=KT)[:, k, 0:LAT]
            if name == "ctx0":
                return (pxl if lo else pxh)[:, :].rearrange("p (k t) -> p k t", k=KT)[:, k, LAT:TOK]
            return (xl if lo else xh)[:, :].rearrange("p (k t) -> p k t", k=KT)[:, k, :]

        def norm_mods(name, k):
            i = norms.index(name)
            layer, which, who = int(name[-1] == "1" and 1), 0 if name[:3] in ("mix", "ctx") else 3, int(name == "ctx0")
            o = C_MODS + 96 * layer + 2 * 8 * which + who
            return small[:, bass.ds(C_A + 8 * i + k, 1)], small[:, bass.ds(o + 2 * k, 1)]

        n_sq, n_sum, n_rs, n_t, n_y = (sem(x) for x in ("n_squares", "n_summed", "n_rstd", "n_scaled", "n_modulated"))
        n_lo, n_self = sem("n_cut"), sem("n_act_self")

        NCUT = {"mix0": 0, "ctx0": KT, "ffn0": 2 * KT, "mix1": 3 * KT, "ffn1": 3 * KT}

        def norm_act(act, name):
            i, T = norms.index(name), NT[name]
            if name == "ctx0":
                act.wait_ge(n_lo, NCUT[name] + 2)
            with act.Fori(0, KT // 2) as t:
                for r in range(2):
                    apart(act)
                    act.wait_ge(n_sum, t * 2 + (KT * i + r + 1))
                    act.activation(nsq[r][:, 0:T], norm_src(name, t * 2 + r), ACT.Square).then_inc(n_sq, 1)
            act.wait_ge(n_sum, KT * (i + 1) + 2)
            act.activation(nrs[:, 0:T], bank(0, 2)[:, 0:T], ACT.Ln, bias=sc(C_EPS), scale=1.0 / D).then_inc(n_self, 1)
            act.wait_ge(n_self, i + 1)
            act.activation(nrs[:, 0:T], nrs[:, 0:T], ACT.Exp, scale=-0.5).then_inc(n_rs, 1)
            act.wait_ge(mods_done, {"mix0": 1, "ctx0": 1, "ffn0": 2, "mix1": 3, "ffn1": 3}[name])
            with act.Fori(0, KT // 2) as t:
                for r in range(2):
                    a, b = norm_mods(name, t * 2 + r)
                    apart(act)
                    if name != "mix1":
                        act.wait_ge(n_lo, t * 2 + (NCUT[name] + r + 1))
                    act.wait_ge(n_t, t * 2 + (KT * i + r + 1))
                    if name == "mix1":
                        act.activation(hinv[:, t * 2 + r, EDGE:EDGE + LAT], nt[r][:, 0:T], ACT.Identity, bias=b, scale=a).then_inc(n_y, 1)
                        continue
                    act.activation(norm_dst(name, t * 2 + r, 0), nt[r][:, 0:T], ACT.Identity, bias=b, scale=a)
                    act.activation(nsq[r][:, 0:T], nt[r][:, 0:T], ACT.Identity, bias=b, scale=a).then_inc(n_y, 1)

        def norm_pe(pe, name):
            i, T = norms.index(name), NT[name]
            need(pe, n_rs, i)
            for k in range(KT):
                pe.wait_ge(n_sq, KT * i + k + 1)
                for o in range(0, T, HALF):
                    w = min(HALF, T)
                    mm = pe.matmul(ps[:, o:o + w], ones[:, :], nsq[k % 2][:, o:o + w], start=k == 0, stop=k == KT - 1)
                mm.then_inc(n_sum, 1)

        def norm_dve(dve, name):
            i, T = norms.index(name), NT[name]
            dve.wait_ge(n_rs, i + 1)
            with dve.Fori(0, KT // 2) as t:
                for r in range(2):
                    dve.wait_ge(n_y, t * 2 + (KT * i + r + 1))
                    dve.tensor_tensor(nt[r][:, 0:T], norm_src(name, t * 2 + r), nrs[:, 0:T], ALU.mult).then_inc(n_t, 1)
                if name != "mix1":
                    for r in range(2):
                        dve.wait_ge(n_y, t * 2 + (KT * i + r + 3))
                        dve.tensor_tensor(norm_dst(name, t * 2 + r, 1), nsq[r][:, 0:T],
                                          norm_dst(name, t * 2 + r, 0).bitcast(F32), ALU.subtract).then_inc(n_lo, 1)

        pieces_lat = [(0, 0, HALF), (1, HALF, HALF)]
        pieces_all = pieces_lat + [(2, LAT, CTX)]
        p_read, p_conv, p_silu, p_sq, p_ss = (sem("p_" + x) for x in ("psum_read", "convolved", "silu", "squared", "summed"))
        p_ssr, p_rs, p_l2, d_self = (sem("p_" + x) for x in ("sums_read", "rstd", "normalised", "dve_self"))
        p_stored = [sem(f"p_stored{i}") for i in range(2)]

        def kind_of(u):
            return "" if u < 0 else "g" if u < U_K else "k" if u < U_Q else "q" if u < U_V else "v" if u < U_Z else "z"

        def conv_pieces(kind):
            return [(0, LAT, CTX), (LAT + 2, CTX, 0)] if kind in "kv" else [(0, HALF, CTX), (HALF, HALF, CTX + HALF)]

        def proj_pe(pe, u, kind):
            pe.wait_ge(w_lo, u.n(1))
            need(pe, p_read, u.n(-1))
            if kind_of(u.base - 2) == "k":
                pe.wait_ge(p_ssr, u.n(-2))
            outs = []
            for b, o, w in (pieces_all if kind in "gkv" else pieces_lat):
                src = lambda t, o=o, w=w: (lambda k: t[:, k * TOK + o:k * TOK + o + w])
                outs.append((ps[:, (3 * u.par + b) * HALF:(3 * u.par + b) * HALF + w], src(pxh), src(pxl)))
            product(pe, u, outs).then_inc(w_used, 1)

        def proj_sums_pe(pe, u, kind):
            pe.wait_ge(p_sq, u.n())
            need(pe, p_ssr, u.n(-1))
            parts = [(6 * HALF, 0, HALF), (7 * HALF, HALF, HALF)]
            if kind == "k":
                parts.append(((3 * u.par + 2) * HALF + CTX, LAT + 2, CTX))
            for at_, o, w in parts:
                mm = pe.matmul(ps[:, at_:at_ + w], ones[:, :], sq[u.par][:, o:o + w], start=True, stop=True)
            mm.then_inc(p_ss, 1)

        def proj_epilogue_act(act, u, kind):
            act.wait_ge(w_used, u.n(1))
            q = bank(3 * u.par, 2)
            qc = ps[:, (3 * u.par + 2) * HALF:(3 * u.par + 2) * HALF + CTX]
            if kind == "g":
                act.activation(grow[:, CTX:TOK], q[0:32, :], ACT.Copy)
                act.activation(grow[:, 0:CTX], qc[0:32, :], ACT.Copy).then_inc(p_read, 1)
                return
            if kind_of(u.base - 2) in ("v", "z"):
                act.wait_ge(p_stored[u.par], u.half(-1) * 32)
            if kind_of(u.base - 2) in ("k", "q"):
                act.wait_ge(p_l2, u.n(-2))
            if kind == "z":
                act.activation(sl[u.par][:, 0:LAT], q, ACT.Silu).then_inc(p_silu, 1)
                act.wait_ge(p_silu, u.n())
                act.sem_inc(p_read, 1)
                return
            need(act, p_conv, u.n(-2))
            mm = act.activation(pad[u.par][:, 2:2 + LAT], q, ACT.Copy)
            if kind != "q":
                mm = act.activation(pad[u.par][:, 4 + LAT:4 + LAT + CTX], qc, ACT.Copy)
            mm.then_inc(p_read, 1)

        def proj_silu_act(act, u, kind):
            act.wait_ge(p_conv, u.n())
            w = LAT if kind == "q" else CONVW
            act.activation(sl[u.par][:, 0:w], acc[u.par][:, 0:w], ACT.Silu).then_inc(p_silu, 1)
            if kind in "kq":
                act.wait_ge(p_silu, u.n())
                need(act, p_ss, u.n(-2))
                act.activation(sq[u.par][:, 0:w], sl[u.par][:, 0:w], ACT.Square).then_inc(p_sq, 1)

        def proj_rstd_act(act, u, kind):
            act.wait_ge(p_ss, u.n())
            need(act, p_l2, u.n(-1))
            w = [(0, LAT, bank(6, 2))]
            if kind == "k":
                at_ = (3 * u.par + 2) * HALF + CTX
                w.append((LAT + 2, CTX, ps[:, at_:at_ + CTX]))
            for o, n, src in w:
                ins = act.activation(rs[:, o:o + n], src, ACT.Ln, bias=sc(C_EPS))
            ins.then_inc(p_ssr, 1)
            act.wait_ge(p_ssr, u.n())
            for o, n, src in w:
                ins = act.activation(rs[:, o:o + n], rs[:, o:o + n], ACT.Exp, scale=-0.5)
            ins.then_inc(p_rs, 1)

        def proj_conv_dve(dve, chain, u, kind):
            dve.wait_ge(p_read, u.n(1))
            need(dve, p_silu, u.n(-2))
            w = LAT if kind == "q" else CONVW
            o = C_CONV + (u.n(-1)) * TAPS
            wt = lambda j: small[:, bass.ds(o + j, 1)]
            a, p_ = acc[u.par], pad[u.par]
            chain(dve.tensor_scalar(a[:, 0:w], p_[:, 0:w], wt(0), None, ALU.mult))
            for j in range(1, TAPS):
                ins = dve.scalar_tensor_tensor(a[:, 0:w], p_[:, j:j + w], wt(j), a[:, 0:w], ALU.mult, ALU.add)
                if j < TAPS - 1:
                    chain(ins)
                else:
                    ins.then_inc(p_conv, 1)

        def proj_l2_dve(dve, u, kind):
            dve.wait_ge(p_rs, u.n())
            need(dve, p_stored[u.par], u.half(-1) * 32)
            w = LAT if kind == "q" else CONVW
            s = float(DK) ** -0.5 if kind == "q" else 1.0
            dve.scalar_tensor_tensor(ob[u.par][:, 0:w], sl[u.par][:, 0:w], s, rs[:, 0:w], ALU.mult, ALU.mult).then_inc(p_l2, 1)

        def proj_store_sp(sp, u, kind):
            if kind in "kq":
                sp.wait_ge(p_l2, u.n())
            else:
                sp.wait_ge(p_silu, u.n())
            src = (ob if kind in "kq" else sl)[u.par]
            dst = {"k": kd, "q": qd, "v": vd, "z": zd}[kind]
            head = u.n(-{"k": U_K, "q": U_Q, "v": U_V, "z": U_Z}[kind])
            for o, w, t in conv_pieces(kind):
                sp.dma_start(dst[head, :, t:t + w], src[:, o:o + w]).then_inc(p_stored[u.par], 16)

        def proj_slots(eng, emit, chain=None, per=None):
            v = 0
            while v <= U_OUT + 1:
                kinds = {kind_of(x) for x in range(v - 3, v + 2)}
                if v >= 3 and len(kinds) == 1 and kind_of(v + 4) == kind_of(v) and v + 4 < U_OUT:
                    with eng.Fori(0, 2) as t:
                        if chain:
                            chain.enter(t, per[kind_of(v)])
                        emit(Unit(v, t))
                        emit(Unit(v + 1, t))
                        if chain:
                            chain.leave(2)
                    v += 4
                else:
                    emit(Unit(v))
                    v += 1

        names = ("k_made kv_scaled v_made r_made dm_ready eq_ready g_exp kk_made t_ready tt_made tt_ready "
                 "xt2_ready z_made z_ready x_made x_ready xt_made xt_ready wt_made wt_ready vn_made vn_ready "
                 "o_made o_added s_made s_ready sg_ready qk_made qk_ready qd_ready cols_ready gu_ready").split()
        q_ = {x: sem("s_" + x) for x in names}
        kv_loaded = [sem(f"kv_loaded{i}") for i in range(2)]
        s_self = {e: sem(f"s_self_{e}") for e in ("dve", "act")}
        heads = range(GH)
        hs = lambda h: slice(h * P, (h + 1) * P)
        v4 = lambda t: t[:, :].rearrange("p (h c) -> p h c", h=GH)
        b4 = lambda b: bank(b).rearrange("p (h c) -> p h c", h=GH)

        def cst(n):
            return cv[:, n, :]

        def cst4(n):
            return cv[:, n:n + 1, :].to_broadcast([P, GH, P])

        def stg(par, d, kind):
            s = stage[par][:, :].rearrange("p (d k h) -> p d k h", d=2, k=CKINDS)
            return s[:, d, kind, :]

        def stg4(par, d, kind):
            s = stage[par][:, :].rearrange("p (d k h x) -> p d k h x", d=2, k=CKINDS, x=1)
            return s[:, d, kind, :, :].to_broadcast([P, GH, P])

        class Half:

            def __init__(self, t, g, lat):
                self.t, self.g, self.lat = t, g, lat
                self.n = t * HG + g + (HG * NCTX if lat else 0)
                self.nl = t * HG + g if lat else None
                if lat:
                    self.chunk = [t + NCTX, t * -1 + (NCHUNK - 1)]
                else:
                    self.chunk = [t, NCTX - 1 - t]

            def c(self, name, d, per=1, k=0):
                return self.n * (2 * per) + (d * per + k + 1)

            def cl(self, name, d):
                return self.nl * 2 + (d + 1 + (2 if name in ("qk_ready", "o_added", "o_made") else 0))

        def scan_load_sp(sp, h):
            need(sp, q_["s_made"], h.n * 2 - 2)
            for d in range(2):
                for nm, src in (("K", kd), ("V", vd)) + ((("Q", qd),) if h.lat else ()):
                    dst = v4(kq[nm, h.g, d])
                    sp.dma_start(dst, src[h.g * GH:(h.g + 1) * GH, :, bass.ds(h.chunk[d] * CHUNK, CHUNK)]
                                 .rearrange("h p c -> p h c")).then_inc(kv_loaded[h.g], 16)

        def loads_done(h):
            return (h.t * 96 + (96 + 64 * NCTX)) if h.lat else (h.t + 1) * 64

        def scan_pe(pe, h):
            g = h.g
            pe.wait_ge(kv_loaded[g], loads_done(h))

            def k_rows(d):
                if h.lat:
                    pe.wait_ge(q_["qk_ready"], h.nl * 2 + 2)
                need(pe, q_["kv_scaled"], h.n * 2)
                for x in heads:
                    mm = pe.transpose(ps[:, d * HALF + x * P:d * HALF + (x + 1) * P], kq["K", g, d][:, hs(x)], cst(K_ID))
                mm.then_inc(q_["k_made"], 1)

            def v_rows(d):
                need(pe, q_["xt_ready"], h.n * (2 * NL))
                if h.lat:
                    pe.wait_ge(q_["o_added"], h.nl * 2 + 2)
                for x in heads:
                    mm = pe.transpose(ps[:, (2 + d) * HALF + x * P:(2 + d) * HALF + (x + 1) * P], kq["V", g, d][:, hs(x)], cst(K_ID))
                mm.then_inc(q_["v_made"], 1)

            def gate_rows(d):
                pe.wait_ge(q_["cols_ready"], h.n + 1)
                pe.wait_ge(q_["s_ready"], h.n * 2 + 4)
                for x in heads:
                    mm = pe.matmul(ps[:, (4 + d) * HALF + x * P:(4 + d) * HALF + (x + 1) * P],
                                   stg(g, d, 0)[:, x:x + 1].to_broadcast([P, P]), cst(K_TRIB if d else K_TRIF), start=True, stop=True)
                mm.then_inc(q_["r_made"], 1)

            def kk(d):
                K = kq["K", g, d]
                need(pe, q_["vn_ready"], h.n * 2)
                for x in heads:
                    mm = pe.matmul(ps[:, (6 + d) * HALF + x * P:(6 + d) * HALF + (x + 1) * P], K[:, hs(x)], K[:, hs(x)],
                                   start=True, stop=True)
                mm.then_inc(q_["kk_made"], 1)

            k_rows(0)
            for d in range(2):
                gate_rows(d)
            v_rows(0)
            k_rows(1)
            v_rows(1)
            for d in range(2):
                kk(d)
            for d in range(2):
                pe.wait_ge(q_["kv_scaled"], h.c("kv_scaled", d))
                pe.wait_ge(q_["t_ready"], h.c("t_ready", d))
                for x in heads:
                    mm = pe.transpose(ps[:, (2 + d) * HALF + x * P:(2 + d) * HALF + (x + 1) * P], tile["TN", d][:, hs(x)], cst(K_ID))
                mm.then_inc(q_["tt_made"], 1)
            if h.lat:
                for d in range(2):
                    for x in heads:
                        mm = pe.matmul(ps[:, d * HALF + x * P:d * HALF + (x + 1) * P], kq["K", g, d][:, hs(x)], kq["Q", g, d][:, hs(x)],
                                       start=True, stop=True)
                    mm.then_inc(q_["qk_made"], 1)
            for l in range(NL):
                for d in range(2):
                    if l == 0:
                        pe.wait_ge(q_["xt2_ready"], h.c("xt2_ready", d))
                        if h.lat:
                            pe.wait_ge(q_["eq_ready"], h.cl("eq_ready", d))
                    else:
                        pe.wait_ge(q_["x_ready"], h.n * (2 * (NL - 1)) + (2 * (l - 1) + d + 1))
                    for x in heads:
                        mm = pe.matmul(ps[:, (4 + d) * HALF + x * P:(4 + d) * HALF + (x + 1) * P], tile["TT", d][:, hs(x)],
                                       tile["X", d][:, hs(x)], start=True, stop=True)
                    mm.then_inc(q_["z_made"], 1)
                for d in range(2):
                    pe.wait_ge(q_["z_ready"], h.n * (2 * NL) + (2 * l + d + 1))
                    if l:
                        pe.wait_ge(q_["xt_ready"], h.n * (2 * NL) + (2 * (l - 1) + d + 1))
                    if l < NL - 1:
                        for x in heads:
                            mm = pe.matmul(ps[:, (6 + d) * HALF + x * P:(6 + d) * HALF + (x + 1) * P], tile["XT", d][:, hs(x)],
                                           tile["Z", d][:, hs(x)], start=True, stop=True)
                        mm.then_inc(q_["x_made"], 1)
                    for x in heads:
                        mm = pe.matmul(ps[:, (2 + d) * HALF + x * P:(2 + d) * HALF + (x + 1) * P], tile["Z", d][:, hs(x)],
                                       tile["XT", d][:, hs(x)], start=True, stop=True)
                    mm.then_inc(q_["xt_made"], 1)
            for d in range(2):
                pe.wait_ge(q_["xt_ready"], h.n * (2 * NL) + (2 * (NL - 1) + d + 1))
                for x in heads:
                    mm = pe.matmul(ps[:, (4 + d) * HALF + x * P:(4 + d) * HALF + (x + 1) * P], tile["Kbe", d][:, hs(x)],
                                   tile["XT", d][:, hs(x)], start=True, stop=True)
                mm.then_inc(q_["wt_made"], 1)
            for d in range(2):
                pe.wait_ge(q_["wt_ready"], h.c("wt_ready", d))
                for x in heads:
                    o = ps[:, (6 + d) * HALF + x * P:(6 + d) * HALF + (x + 1) * P]
                    pe.matmul(o, tile["XT", d][:, hs(x)], tile["Vb", d][:, hs(x)], start=True, stop=False)
                    mm = pe.matmul(o, tile["WTn", d][:, hs(x)], S[g, d][:, hs(x)], start=False, stop=True)
                mm.then_inc(q_["vn_made"], 1)
            for d in range(2):
                pe.wait_ge(q_["vn_ready"], h.c("vn_ready", d))
                if h.lat:
                    pe.wait_ge(q_["qd_ready"], h.cl("qd_ready", d))
                    pe.wait_ge(q_["qk_ready"], h.cl("qk_ready", d))
                    for x in heads:
                        o = ps[:, (2 + d) * HALF + x * P:(2 + d) * HALF + (x + 1) * P]
                        pe.matmul(o, S[g, d][:, hs(x)], tile["QdT", d][:, hs(x)], start=True, stop=False)
                        mm = pe.matmul(o, tile["VN", d][:, hs(x)], tile["qkT", d][:, hs(x)], start=False, stop=True)
                    mm.then_inc(q_["o_made"], 1)
                for x in heads:
                    mm = pe.matmul(ps[:, (4 + d) * HALF + x * P:(4 + d) * HALF + (x + 1) * P], tile["Kdec", d][:, hs(x)],
                                   tile["VN", d][:, hs(x)], start=True, stop=True)
                mm.then_inc(q_["s_made"], 1)

        def scan_act(act, h):
            g = h.g
            for d in range(2):
                G = tile["G", d]
                act.wait_ge(q_["dm_ready"], h.c("dm_ready", d))
                act.activation(G[:, :], G[:, :], ACT.Abs).then_inc(s_self["act"], 1)
                act.wait_ge(s_self["act"], h.n * 2 + d + 1)
                act.activation(G[:, :], G[:, :], ACT.Exp, scale=-1.0).then_inc(q_["g_exp"], 1)
            if h.lat:
                act.wait_ge(q_["o_made"], h.nl * 2 + 2)
                for d in range(2):
                    act.activation(tile["QdT", d][:, :], bank(4 + d), ACT.Exp).then_inc(q_["eq_ready"], 1)
            for d in range(2):
                act.wait_ge(q_["tt_made"], h.c("tt_made", d))
                act.activation(tile["TT", d][:, :], bank(2 + d), ACT.Copy).then_inc(q_["tt_ready"], 1)
            for l in range(NL):
                for d in range(2):
                    if l < NL - 1:
                        act.wait_ge(q_["x_made"], h.n * (2 * (NL - 1)) + (2 * l + d + 1))
                        act.activation(tile["X", d][:, :], bank(6 + d), ACT.Copy).then_inc(q_["x_ready"], 1)
                    act.wait_ge(q_["xt_made"], h.n * (2 * NL) + (2 * l + d + 1))
                    act.activation(tile["XT", d][:, :], bank(2 + d), ACT.Copy).then_inc(q_["xt_ready"], 1)
            for d in range(2):
                act.wait_ge(q_["wt_made"], h.c("wt_made", d))
                act.activation(tile["WTn", d][:, :], bank(4 + d), ACT.Copy, scale=-1.0).then_inc(q_["wt_ready"], 1)
            for d in range(2):
                act.wait_ge(q_["vn_made"], h.c("vn_made", d))
                act.activation(tile["VN", d][:, :], bank(6 + d), ACT.Copy).then_inc(q_["vn_ready"], 1)

        def scan_pool(pool, h):
            g = h.g
            for d in range(2):
                G, GU = tile["G", d], tile["GU", d]
                pool.wait_ge(q_["g_exp"], h.c("g_exp", d))
                if h.lat:
                    pool.wait_ge(q_["qk_ready"], h.nl * 2 + 2)
                    pool.tensor_tensor(v4(GU), v4(G), cst4(K_QKB if d else K_QKF), ALU.mult).then_inc(q_["gu_ready"], 1)
            for d in range(2):
                pool.wait_ge(q_["s_ready"], h.n * 2 + 4)
                pool.tensor_tensor(v4(tile["Sg", d]), v4(S[g, d]), stg4(g, d, 5), ALU.mult).then_inc(q_["sg_ready"], 1)

        def stage_cols(dve, h):
            for d in range(2):
                s = stage[h.g][:, d * CKINDS * GH:(d + 1) * CKINDS * GH]
                n = CKINDS * GH
                src = col[:, bass.ds(h.chunk[d] * (2 * HG * n) + (d * HG * n + h.g * n), n)]
                ins = dve.tensor_copy(s, src)
            ins.then_inc(q_["cols_ready"], 1)

        def scan_dve(dve, h):
            g = h.g
            stage_cols(dve, h)
            dve.wait_ge(q_["cols_ready"], h.n + 1)

            def keys(d):
                dve.wait_ge(q_["k_made"], h.c("k_made", d))
                dve.tensor_tensor(v4(tile["Kbe", d]), b4(d), stg4(g, d, 3), ALU.mult)
                dve.tensor_tensor(v4(tile["Kdec", d]), b4(d), stg4(g, d, 4), ALU.mult)

            def values(d):
                dve.wait_ge(q_["v_made"], h.c("v_made", d))
                dve.tensor_tensor(v4(tile["Vb", d]), b4(2 + d), stg4(g, d, 2), ALU.mult).then_inc(q_["kv_scaled"], 1)

            keys(0)
            for d in range(2):
                dve.wait_ge(q_["r_made"], h.c("r_made", d))
                dve.tensor_tensor(v4(tile["G", d]), b4(4 + d), stg4(g, d, 1), ALU.subtract).then_inc(q_["dm_ready"], 1)
            values(0)
            keys(1)
            values(1)
            steps = 4

            def own(d, n):
                dve.wait_ge(s_self["dve"], h.n * (2 * steps) + (2 * n + d + 1))
            for d in range(2):
                dve.wait_ge(q_["g_exp"], h.c("g_exp", d))
                dve.tensor_tensor(v4(tile["GL", d]), v4(tile["G", d]), cst4(K_NB if d else K_NF), ALU.mult).then_inc(s_self["dve"], 1)
            for d in range(2):
                own(d, 0)
                dve.tensor_tensor(v4(tile["GL", d]), v4(tile["GL", d]), stg4(g, d, 2), ALU.mult).then_inc(s_self["dve"], 1)
            for d in range(2):
                own(d, 1)
                dve.wait_ge(q_["kk_made"], h.c("kk_made", d))
                dve.tensor_tensor(v4(tile["TN", d]), b4(6 + d), v4(tile["GL", d]), ALU.mult).then_inc(s_self["dve"], 1)
            for d in range(2):
                own(d, 2)
                dve.tensor_tensor(v4(tile["TN", d]), v4(tile["TN", d]), cst4(K_ID), ALU.add).then_inc(s_self["dve"], 1)
            for d in range(2):
                own(d, 3)
                dve.tensor_tensor(v4(tile["X", d]), v4(tile["TN", d]), cst4(K_LB if d else K_LF), ALU.mult).then_inc(q_["t_ready"], 1)
            for d in range(2):
                dve.wait_ge(q_["tt_ready"], h.c("tt_ready", d))
                dve.tensor_tensor(v4(tile["XT", d]), v4(tile["TT", d]), cst4(K_LF if d else K_LB), ALU.mult).then_inc(q_["xt2_ready"], 1)
            for l in range(NL):
                for d in range(2):
                    dve.wait_ge(q_["z_made"], h.n * (2 * NL) + (2 * l + d + 1))
                    dve.tensor_tensor(v4(tile["Z", d]), b4(4 + d), cst4((K_LB if d else K_LF) + 1 + l), ALU.mult).then_inc(q_["z_ready"], 1)
                if h.lat and l < 2:
                    d = l
                    if l == 0:
                        dve.wait_ge(kv_loaded[g], loads_done(h))
                    dve.wait_ge(q_["eq_ready"], h.cl("eq_ready", d))
                    dve.tensor_tensor(v4(tile["QdT", d]), v4(tile["QdT", d]), v4(kq["Q", g, d]), ALU.mult).then_inc(q_["qd_ready"], 1)
                    dve.wait_ge(q_["gu_ready"], h.cl("gu_ready", d))
                    dve.wait_ge(q_["qk_made"], h.cl("qk_made", d))
                    dve.tensor_tensor(v4(tile["qkT", d]), b4(d), v4(tile["GU", d]), ALU.mult).then_inc(q_["qk_ready"], 1)
            for d in range(2):
                if h.lat:
                    dve.wait_ge(q_["o_made"], h.cl("o_made", d))
                dve.wait_ge(q_["s_made"], h.c("s_made", d))
                dve.wait_ge(q_["sg_ready"], h.c("sg_ready", d))
                dve.tensor_tensor(v4(S[g, d]), b4(4 + d), v4(tile["Sg", d]), ALU.add).then_inc(q_["s_ready"], 1)
                if h.lat:
                    dve.wait_ge(q_["o_added"], h.nl * 2 + (2 + d))
                    o = oTv[:, g * GH:(g + 1) * GH, bass.ds((h.chunk[d] - NCTX) * CHUNK, CHUNK)]
                    dve.tensor_tensor(o, b4(2 + d), o, ALU.add).then_inc(q_["o_added"], 1)

        def scan(eng, emit):
            for t in range(NCTX):
                for g in range(HG):
                    emit(eng, Half(t, g, False))
            with eng.Fori(0, NLAT) as t:
                for g in range(HG):
                    emit(eng, Half(t, g, True))

        r_z = [sem(f"r_z{i}") for i in range(2)]
        r_sq, r_sum, r_rs, r_y, r_h, r_lo, r_self = (sem("r_" + x) for x in ("squares", "summed", "rstd", "gated", "hi", "cut", "self"))
        r_added, r_sc = sem("r_added"), sem("r_scaled")

        f_pad, f_conv, f_silu, f_hid = (sem("f_" + x) for x in ("padded", "convolved", "silu", "hidden"))
        d_hi, d_lo, d_added = sem("d_hi"), sem("d_lo"), sem("d_added")
        h_saved, h_back = sem("h_saved"), sem("h_back")

        def gu_unit(L, J, w, t):
            class G4(Unit):
                def n(s, off=0):
                    v = s.base + off
                    return v if s.trip is None else s.trip * 4 + v

                def half(s, off=0):
                    v = (s.base + off) // 2
                    return v if s.trip is None else s.trip * 2 + v

                def plus(s, k):
                    return G4(s.base + k, s.trip)
            return G4(U_GU[L] + 2 * J + w, t)

        def pairs(eng, L, emit, chain=None):
            emit(L, 0, None)
            with eng.Fori(0, (FT - 2) // 2) as t:
                if chain:
                    chain.enter(t, 2 * (FTAPS - 1))
                emit(L, 1, t)
                emit(L, 2, t)
                if chain:
                    chain.leave((FT - 2) // 2)
            emit(L, FT - 1, None)
            emit(L, FT, None)

        def jn(J, t, off=0, mul=1):
            v = (J + off) * mul
            return v if t is None else t * (2 * mul) + v

        def up_pe(pe):
            def emit(L, J, t):
                if J == FT:
                    return
                for w in range(2):
                    u = gu_unit(L, J, w, t)
                    pe.wait_ge(w_lo, u.n(1))
                    b = 4 * (J % 2) + 2 * w
                    v = jn(J, t, -1 + FT * L)
                    if not (t is None and J < 2):
                        pe.wait_ge(f_hid if w else f_pad, v)
                    outs = [(bank(b + i), (lambda i: lambda k: xh[:, k * LAT + i * HALF:k * LAT + (i + 1) * HALF])(i),
                             (lambda i: lambda k: xl[:, k * LAT + i * HALF:k * LAT + (i + 1) * HALF])(i)) for i in range(2)]
                    product(pe, u, outs).then_inc(w_used, 1)
            return emit

        def up_act(act):
            def emit(L, J, t):
                if J < FT:
                    cut_hi(act, gu_unit(L, J, 1, t))
                if not (t is None and J == 0):
                    g0 = gu_unit(L, J - 1, 0, t)
                    act.wait_ge(w_used, g0.n(1))
                    need(act, f_conv, jn(J, t, -1 + FT * L))
                    act.activation(fpad[:, 1:1 + LAT], bank(4 * ((J - 1) % 2), 2), ACT.Copy).then_inc(f_pad, 1)
                    apart(act)
                    act.wait_ge(f_conv, jn(J, t, FT * L))
                    need(act, f_hid, jn(J, t, -1 + FT * L))
                    act.activation(fsl[:, :], facc[:, :], ACT.Silu,
                                   bias=small[:, bass.ds(jn(J, t, C_FBIAS + FT * L - 1), 1)]).then_inc(f_silu, 1)
                if J < FT - 1:
                    cut_hi(act, gu_unit(L, J + 1, 0, t))
            return emit

        def up_dve(dve, chain):
            def emit(L, J, t):
                if J < FT:
                    cut_lo(dve, gu_unit(L, J, 1, t))
                if not (t is None and J == 0):
                    dve.wait_ge(f_pad, jn(J, t, FT * L))
                    need(dve, f_silu, jn(J, t, -1 + FT * L))
                    o = jn(J, t, FT * L - 1, FTAPS)
                    wt = lambda j: small[:, bass.ds(o + (C_FCONV + j), 1)]
                    chain(dve.tensor_scalar(facc[:, :], fpad[:, 0:LAT], wt(0), None, ALU.mult))
                    chain(dve.scalar_tensor_tensor(facc[:, :], fpad[:, 1:1 + LAT], wt(1), facc[:, :], ALU.mult, ALU.add))
                    dve.scalar_tensor_tensor(facc[:, :], fpad[:, 2:2 + LAT], wt(2), facc[:, :], ALU.mult, ALU.add).then_inc(f_conv, 1)
                    dve.wait_ge(f_silu, jn(J, t, FT * L))
                    dve.wait_ge(w_used, gu_unit(L, J - 1, 1, t).n(1))
                    dve.tensor_tensor(hidv[:, jn(J, t, -1), :], bank(4 * ((J - 1) % 2) + 2, 2), fsl[:, :], ALU.mult).then_inc(f_hid, 1)
                if J < FT - 1:
                    cut_lo(dve, gu_unit(L, J + 1, 0, t))
            return emit

        def down_unit(L, half, k, t):
            return Unit(U_DN[L] + FT * half + k, t)

        def downs(eng, L, half, emit):
            for k in range(2):
                emit(L, half, k, None)
            with eng.Fori(0, (FT - 4) // 2) as t:
                emit(L, half, 2, t)
                emit(L, half, 3, t)
            for k in (FT - 2, FT - 1):
                emit(L, half, k, None)

        def dn(L, half, k, t, off=0):
            v = FT * (2 * L + half) + k + off
            return v if t is None else t * 2 + v

        def down_pe(pe):
            def emit(L, half, k, t):
                u = down_unit(L, half, k, t)
                pe.wait_ge(w_lo, u.n(1))
                pe.wait_ge(d_lo, dn(L, half, k, t, 1))
                for m in range(KT):
                    if t is None and k == 0 and (half or L):
                        pe.wait_ge(d_added, KT * (2 * L + half - 1) + m + 1)
                    w = slice(m * P, (m + 1) * P)
                    for n, (a, b) in enumerate(((wh, dxh), (wh, dxl), (wl, dxh))):
                        mm = pe.matmul(bank(m), a[u.par][:, w], b[k % 2][:, :], start=t is None and k == 0 and n == 0,
                                       stop=t is None and k == FT - 1 and n == 2)
                mm.then_inc(w_used, 1)
            return emit

        def down_cut_act(act, L, half, k, t):
            u = down_unit(L, half, k, t)
            cut_hi(act, u)
            apart(act)
            act.activation(dxh[k % 2][:, :], hidv[:, k if t is None else t * 2 + k, half * HALF:(half + 1) * HALF], ACT.Copy).then_inc(d_hi, 1)

        def down_cut_dve(dve, L, half, k, t):
            cut_lo(dve, down_unit(L, half, k, t))
            dve.wait_ge(d_hi, dn(L, half, k, t, 1))
            dve.tensor_tensor(dxl[k % 2][:, :], hidv[:, k if t is None else t * 2 + k, half * HALF:(half + 1) * HALF],
                              dxh[k % 2][:, :].bitcast(F32), ALU.subtract).then_inc(d_lo, 1)

        def down_dve(dve, L):
            def epilogue(half):
                for m in range(KT):
                    dve.wait_ge(w_used, U_DN[L] + FT * (half + 1))
                    dve.wait_ge(h_back, 16 * (L + 1))
                    h = h2v[:, m, half * HALF:(half + 1) * HALF]
                    dve.scalar_tensor_tensor(h, bank(m), mod(L, 5, m, 0), h, ALU.mult, ALU.add).then_inc(d_added, 1)
            def with_ada(half, base, row, t):
                for q in range(4):
                    down_cut_dve(dve, L, half, base + q, t * 2)
                    dve.wait_ge(piece_loaded[q % 2], t * 32 + 16 * (2 * row + q // 2 + 1))
                    dve.wait_ge(piece_used, t * 4 + (4 * row + q + 1))
                    a = acc1[:, q * PIECE:(q + 1) * PIECE]
                    dve.scalar_tensor_tensor(a, adap[q % 2][:, :], small[:, bass.ds(t * 2 + (C_SILU + 2 * row), 1)], a,
                                             ALU.mult, ALU.add).then_inc(piece_used, 1)

            def plain(half, base, trips):
                with dve.Fori(0, trips) as t:
                    for k in range(2):
                        down_cut_dve(dve, L, half, base + k, t)

            if L == 0:
                dve.wait_ge(piece_zero, 1)
                with dve.Fori(0, ROWS0) as t:
                    with_ada(0, 0, 0, t)
                plain(0, 4 * ROWS0, (FT - 4 * ROWS0) // 2)
            else:
                plain(0, 0, FT // 2)
            for k in range(2):
                down_cut_dve(dve, L, 1, k, None)
            epilogue(0)
            if L == 0:
                with dve.Fori(0, KT - ROWS0) as t:
                    with_ada(1, 2, ROWS0, t)
                plain(1, 2 + 4 * (KT - ROWS0), (FT - 2 - 4 * (KT - ROWS0)) // 2)
            else:
                plain(1, 2, FT // 2 - 1)
            epilogue(1)

        def pool_dve(dve):
            self_n = [0]

            def step(ins):
                self_n[0] += 1
                ins.then_inc(pl_self, 1)
                dve.wait_ge(pl_self, self_n[0])

            def cut(k):
                dve.wait_ge(pl_hi, k + 1)
                dve.tensor_tensor(pll[:, k * LAT:(k + 1) * LAT], pd[k % 2][:, :], plh[:, k * LAT:(k + 1) * LAT].bitcast(F32),
                                  ALU.subtract).then_inc(pl_lo, 1)
            for k in range(KT):
                need(dve, pl_d, k)
                need(dve, pl_lo, k - 1)
                gi = k // 2
                win = POOL_WINDOWS[gi]
                src, lo, hi, reach = hinv[:, k, :], 0, PW, 1
                n = 0
                while 2 ** n < win:
                    a, b = (1, 0) if n == 0 else (reach, reach)
                    lo, hi = lo + a, hi - b
                    dst = pt[n % 2]
                    step(dve.tensor_tensor(dst[:, lo:hi], src[:, lo - a:hi - a], src[:, lo + b:hi + b], ALU.add))
                    if n:
                        reach *= 2
                    src = dst
                    n += 1
                for side in range(2):
                    o = EDGE + side * (LAT - EDGE)
                    step(dve.tensor_tensor(src[:, o:o + EDGE], src[:, o:o + EDGE], sc(C_EDGE + 2 * EDGE * gi + EDGE * side, EDGE), ALU.mult))
                dve.scalar_tensor_tensor(pd[k % 2][:, :], src[:, EDGE:EDGE + LAT], 1.0 / win, hinv[:, k, EDGE:EDGE + LAT],
                                         ALU.mult, ALU.subtract).then_inc(pl_d, 1)
                if k:
                    cut(k - 1)
            cut(KT - 1)
            for w in range(2):
                cut_lo(dve, Unit(U_POOL + w))
            for m in range(KT):
                dve.wait_ge(w_used, U_POOL + m // 4 + 1)
                dve.scalar_tensor_tensor(h3v[:, m, :], bank(2 * (m % 4), 2), sc(C_PG + m), h2v[:, m, :],
                                         ALU.mult, ALU.add).then_inc(pl_added, 1)

        def pool_pe(pe):
            for m in range(KT):
                u = Unit(U_POOL + m // 4)
                pe.wait_ge(w_lo, u.n(1))
                pe.wait_ge(pl_lo, 2 * (m // 2) + 2)
                need(pe, pl_added, m - 3)
                for kk in range(2):
                    o = (2 * (m % 4) + kk) * P
                    k = 2 * (m // 2) + kk
                    for n, (a, b) in enumerate(((wh, plh), (wh, pll), (wl, plh))):
                        for i in range(2):
                            mm = pe.matmul(bank(2 * (m % 4) + i), a[u.par][:, o:o + P], b[:, k * LAT + i * HALF:k * LAT + (i + 1) * HALF],
                                           start=kk == 0 and n == 0, stop=kk == 1 and n == 2)
                if m % 4 == 3:
                    mm.then_inc(w_used, 1)

        f_self2 = sem("f_dve_self")
        fchain = Chain(None, f_self2)

        x_loaded, const_loaded = sem("x_loaded"), sem("const_loaded")
        ada_loaded = [sem(f"ada_loaded{i}") for i in range(KT // 2)]
        late_loaded = [sem(f"ada_late_loaded{i}") for i in range(2)]
        piece_loaded = [sem(f"ada_piece_loaded{i}") for i in range(2)]
        ada_silu, ada_made, ada_copied, ada_turned = (sem("ada_" + x) for x in ("silu", "made", "copied", "turned"))
        late_used, late_summed = sem("ada_late_used"), sem("ada_late_summed")
        piece_used, piece_zero = sem("ada_piece_used"), sem("ada_piece_zero")
        mods_self = sem("mods_self")
        out_stored = sem("out_stored")
        g_dve, g_act, g_pe, g_lift = sem("g_dve"), sem("g_act"), sem("g_pe"), sem("g_lift")
        pl_self, pl_d, pl_hi, pl_lo, pl_added = (sem("pl_" + x) for x in ("self", "pooled", "hi", "cut", "added"))

        @block.sync
        def _(sp):
            sp.dma_start(small[:, 0:N_IN], small_in).then_inc(start_loaded, 16)
            sp.dma_start(fixed[:, :], const_in[:, 0:2 * P]).then_inc(start_loaded, 16)
            sp.dma_start(hTv, xT.rearrange("k p t -> p k t")).then_inc(x_loaded, 16)
            sp.dma_start(ctxv, ctxT.rearrange("k p t -> p k t")).then_inc(x_loaded, 16)
            for i in range(KT // 2):
                sp.dma_start(adae[i][:, :].rearrange("p (k c) -> p k c", k=2),
                             ada_w[0, 2 * i * P:2 * (i + 1) * P, 0:EARLY].rearrange("(k p) c -> p k c", k=2)).then_inc(ada_loaded[i], 16)
            load_unit(sp, Unit(0))
            load_unit(sp, Unit(1))

            def slot(v):
                if v.base < U_OUT:
                    load_unit(sp, v.plus(2))
                if U_K <= v.base - 2 < U_OUT:
                    proj_store_sp(sp, v.plus(-2), kind_of(v.base - 2))
            proj_slots(sp, slot)
            for r in range(2):
                sp.wait_ge(p_stored[r], 32 * (U_OUT - U_K) // 2)
            sp.wait_ge(phase_end, 4 * 3)
            sp.dma_start(const[:, :], const_in).then_inc(const_loaded, 16)
            scan(sp, scan_load_sp)
            sp.wait_ge(phase_end, 4 * 5)
            for h in range(HEADS):
                need(sp, r_y, h - 1)
                sp.dma_start(zt[h % 2][:, :], zd[h, :, CTX:TOK]).then_inc(r_z[h % 2], 16)
            sp.wait_ge(phase_end, 4 * 6)
            for u in range(U_OUT + 2, U_OUT + KT):
                load_unit(sp, Unit(u))
                for k in {2: (0, 1), 3: (2, 3), 4: (4,), 5: (5,), 6: (6,), 7: (7,)}[u - U_OUT]:
                    need(sp, late_used, k - 1)
                    sp.dma_start(adal[k % 2][:, :], ada_w[0, k * P:(k + 1) * P, EARLY:]).then_inc(late_loaded[k % 2], 16)
            for L in range(2):
                for w in range(2):
                    load_unit(sp, Unit(U_GU[L] + w), W_GU[L] + w)
                sp.wait_ge(phase_end, 4 * (7 if L == 0 else 12))
                sp.dma_start(hd.rearrange("k p t -> p k t"), h3v if L else hTv).then_inc(h_saved, 16)
                with sp.Fori(0, FT - 1) as t:
                    for w in range(2):
                        load_unit(sp, Unit(U_GU[L] + 2 + w, t), t * 2 + (W_GU[L] + 2 + w))
                for half in range(2):
                    with sp.Fori(0, FT // 2) as t:
                        for w in range(2):
                            load_unit(sp, Unit(U_DN[L] + FT * half + w, t), t * 2 + (W_DN[L] + w))
                if L == 0:
                    for w in range(2):
                        load_unit(sp, Unit(U_POOL + w), W_POOL + w)
            sp.wait_ge(phase_end, 4 * 15)
            sp.dma_start(outT.rearrange("k p t -> p k t"), h2v).then_inc(out_stored, 16)
            sp.wait_ge(out_stored, 16)

        @block.gpsimd
        def _(pool):
            meet(pool, 1)
            for i in range(2):
                for o, w in ((0, 2), (2 + LAT, 2), (4 + LAT + CTX, 2)):
                    pool.memset(pad[i][:, o:o + w], 0.0)
            pool.memset(rs[:, LAT:LAT + 2], 0.0)
            meet(pool, 2)
            meet(pool, 3)
            pool.memset(oT[:, :], 0.0)
            pool.wait_ge(const_loaded, 16)
            meet(pool, 4)
            scan(pool, scan_pool)
            for n in (5, 6, 7):
                meet(pool, n)
            pool.wait_ge(h_saved, 16)
            meet(pool, 8)
            meet(pool, 9)
            pool.dma_start(h2v, hd.rearrange("k p t -> p k t")).then_inc(h_back, 16)
            pool.memset(acc1[:, :], 0.0).then_inc(piece_zero, 1)
            for n in range(KT * PIECES):
                if n >= 2:
                    pool.wait_ge(piece_used, 4 + n - 1)
                k, c = n // PIECES, (n % PIECES) * PIECE
                pool.dma_start(adap[n % 2][:, :], ada_w[1, k * P:(k + 1) * P, c:c + PIECE]).then_inc(piece_loaded[n % 2], 16)
            meet(pool, 10)
            for e in (0, EDGE + LAT):
                pool.memset(hinv[:, :, e:e + EDGE], 0.0)
            for n in (11, 12):
                meet(pool, n)
            pool.wait_ge(h_saved, 32)
            for n in (13, 14):
                meet(pool, n)
            pool.dma_start(h2v, hd.rearrange("k p t -> p k t")).then_inc(h_back, 16)
            meet(pool, 15)

        @block.scalar
        def _(act):
            act.wait_ge(start_loaded, 32)
            act.sem_inc(n_y, 2)
            act.activation(sc(C_SILU, 2 * KT), sc(C_COND, 2 * KT), ACT.Silu).then_inc(ada_silu, 1)
            act.activation(sc(C_ALOG, 16), sc(C_ALOG, 16), ACT.Exp)
            act.wait_ge(x_loaded, 32)
            norm_act(act, "mix0")
            norm_act(act, "ctx0")
            meet(act, 1)
            cut_hi(act, Unit(0))

            def slot(v):
                if v.base + 1 < U_OUT:
                    cut_hi(act, v.plus(1))
                if 0 <= v.base - 1 < U_OUT:
                    proj_epilogue_act(act, v.plus(-1), kind_of(v.base - 1))
                if U_K <= v.base - 2 < U_V:
                    proj_rstd_act(act, v.plus(-2), kind_of(v.base - 2))
                if U_K <= v.base - 1 < U_Z:
                    proj_silu_act(act, v.plus(-1), kind_of(v.base - 1))
            meet(act, 2)
            proj_slots(act, slot)
            meet(act, 3)
            act.wait_ge(g_dve, 1)
            act.activation(ga[1][:, :], ga[0][:, :], ACT.Abs).then_inc(g_act, 1)
            act.wait_ge(g_act, 1)
            act.activation(ga[1][:, :], ga[1][:, :], ACT.Exp, scale=-1.0).then_inc(g_act, 1)
            act.wait_ge(g_lift, 2)
            tab = col[:, :].rearrange("p (x k) -> p x k", k=CKINDS * GH)[:, :, 2 * GH:]
            act.activation(tab, tab, ACT.Exp)
            meet(act, 4)
            scan(act, scan_act)
            meet(act, 5)
            for h in range(HEADS + 1):
                if h < HEADS:
                    need(act, r_sum, h - 1)
                    act.activation(rsq[h % 2][:, :], oTv[:, h, :], ACT.Square).then_inc(r_sq, 1)
                if h:
                    g = h - 1
                    act.wait_ge(r_sum, g + 1)
                    need(act, r_y, g - 1)
                    act.activation(rrs[g % 2][:, :], bank(2 * (g % 2), 2), ACT.Ln, bias=sc(C_EPS), scale=1.0 / DK).then_inc(r_self, 1)
                    act.wait_ge(r_self, g + 1)
                    act.activation(rrs[g % 2][:, :], rrs[g % 2][:, :], ACT.Exp, scale=-0.5).then_inc(r_rs, 1)
                    act.wait_ge(r_y, g + 1)
                    act.activation(yh[:, g * LAT:(g + 1) * LAT], rt[g % 2][:, :], ACT.Copy).then_inc(r_h, 1)
            meet(act, 6)
            for m in range(KT):
                cut_hi(act, Unit(U_OUT + m))
            meet(act, 7)
            norm_act(act, "ffn0")
            cut_hi(act, gu_unit(0, 0, 0, None))
            meet(act, 8)
            pairs(act, 0, up_act(act))
            meet(act, 9)
            for half in range(2):
                with act.Fori(0, FT // 2) as t:
                    for k in range(2):
                        down_cut_act(act, 0, half, k, t)
            meet(act, 10)
            norm_act(act, "mix1")
            meet(act, 11)
            for k in range(KT):
                act.wait_ge(pl_d, k + 1)
                act.activation(plh[:, k * LAT:(k + 1) * LAT], pd[k % 2][:, :], ACT.Copy).then_inc(pl_hi, 1)
            for w in range(2):
                cut_hi(act, Unit(U_POOL + w))
            meet(act, 12)
            norm_act(act, "ffn1")
            cut_hi(act, gu_unit(1, 0, 0, None))
            meet(act, 13)
            pairs(act, 1, up_act(act))
            meet(act, 14)
            for half in range(2):
                with act.Fori(0, FT // 2) as t:
                    for k in range(2):
                        down_cut_act(act, 1, half, k, t)
            meet(act, 15)

        @block.vector
        def _(dve):
            chain = Chain(dve, d_self)

            def small_mod(layer, which, who):
                o = C_MODS + 96 * layer + 16 * which
                return small[:, o:o + 16].rearrange("p (k w) -> p k w", w=2)[:, :, who]

            def modulators(which):
                for i in which:
                    layer, m, who, w = ((0, 1, 0, C_NMIX), (0, 1, 1, C_NMIX), (0, 4, 0, C_NFFN),
                                        (1, 1, 0, C_NMIX + KT), (1, 4, 0, C_NFFN + KT))[i]
                    dve.scalar_tensor_tensor(sc(C_A + KT * i, KT), small_mod(layer, m, who), 1.0, sc(w, KT),
                                             ALU.add, ALU.mult).then_inc(mods_self, 1)
                    dve.wait_ge(mods_self, (2, 3, 5, 7, 8)[i])

            def late_mods(layer, first, after):
                n = 48 - first
                o = C_MODS + 96 * layer + 2 * first
                b = C_ADAB + 48 * layer + first
                dve.wait_ge(late_summed, layer + 1)
                out = small[:, o:o + 2 * n].rearrange("p (m w) -> p m w", w=2)[:, :, 0]
                dve.tensor_tensor(out, ps[:, 4 * HALF:4 * HALF + n], sc(b, n), ALU.add).then_inc(mods_self, 1)
                dve.wait_ge(mods_self, after)

            fchain.eng = dve
            dve.sem_inc(n_lo, 2)
            dve.sem_inc(piece_used, 4)
            dve.wait_ge(start_loaded, 32)
            dve.wait_ge(ada_made, 1)
            dve.tensor_copy(mrow[:, :], ps[0:2, 2 * HALF:2 * HALF + EARLY]).then_inc(ada_copied, 1)
            dve.wait_ge(ada_turned, 1)
            out = small[:, C_MODS:C_MODS + 48].rearrange("p (m w) -> p m w", w=2)
            src = ps[:, 2 * HALF:2 * HALF + 48].rearrange("p (m w) -> p m w", w=2)
            ab = small[:, C_ADAB:C_ADAB + 24].rearrange("p (m w) -> p m w", w=1).to_broadcast([P, 24, 2])
            dve.tensor_tensor(out, src, ab, ALU.add).then_inc(mods_self, 1)
            dve.wait_ge(mods_self, 1)
            modulators((0, 1))
            dve.sem_inc(mods_done, 1)
            dve.wait_ge(x_loaded, 32)
            norm_dve(dve, "mix0")
            norm_dve(dve, "ctx0")
            meet(dve, 1)
            cut_lo(dve, Unit(0))
            meet(dve, 2)

            def slot(v):
                if v.base + 1 < U_OUT:
                    cut_lo(dve, v.plus(1))
                if U_K <= v.base - 1 < U_Z:
                    proj_conv_dve(dve, chain, v.plus(-1), kind_of(v.base - 1))
                if U_K <= v.base - 2 < U_V:
                    proj_l2_dve(dve, v.plus(-2), kind_of(v.base - 2))
            n = 2 * (TAPS - 1)
            proj_slots(dve, slot, chain, {"k": n, "q": n, "v": n, "z": 0})
            meet(dve, 3)
            y, e, s_, s2, den, out = (t[:, :].rearrange("p (n c) -> p n c", n=NCHUNK) for t in ga)
            dve.wait_ge(g_pe, 1)
            raw = ps[:, 0:GN].rearrange("p (n c) -> p n c", n=NCHUNK)
            dt = small[:, C_DT:C_DT + 16].rearrange("p (x c) -> p x c", x=1).to_broadcast([P, NCHUNK, 16])
            ea = small[:, C_ALOG:C_ALOG + 16].rearrange("p (x c) -> p x c", x=1).to_broadcast([P, NCHUNK, 16])
            dve.tensor_scalar(y[:, :, 0:16], raw[:, :, 0:16], -1.0, None, ALU.mult)
            dve.tensor_tensor(y[:, :, 16:32], raw[:, :, 16:32], dt, ALU.add).then_inc(g_dve, 1)
            dve.wait_ge(g_act, 2)
            gs = [1]

            def gstep(ins):
                gs[0] += 1
                ins.then_inc(g_dve, 1)
                dve.wait_ge(g_dve, gs[0])
            gstep(dve.tensor_scalar(den, e, 2.0, None, ALU.add))
            gstep(dve.reciprocal(den, den))
            gstep(dve.tensor_tensor(s_, e, den, ALU.mult))
            gstep(dve.tensor_tensor(s2, s_, s_, ALU.mult))
            gstep(dve.tensor_scalar(den, s2, 1.0 / 17, None, ALU.mult))
            for k in range(15, 1, -2):
                gstep(dve.scalar_tensor_tensor(den, den, 1.0 / k, s2, ALU.add, ALU.mult))
            gstep(dve.scalar_tensor_tensor(den, den, 1.0, s_, ALU.add, ALU.mult))
            gstep(dve.tensor_scalar(s_, y, 0.0, None, ALU.max))
            gstep(dve.scalar_tensor_tensor(out, den, 2.0, s_, ALU.mult, ALU.add))
            gstep(dve.tensor_scalar(y[:, :, 0:16], out[:, :, 0:16], -1.0, None, ALU.mult))
            gstep(dve.scalar_tensor_tensor(y[:, :, 16:32], out[:, :, 16:32], -1.0, ea, ALU.mult, ALU.mult))
            kind = lambda d, k: colv[:, :, d, :, k, :]
            lift = lambda t, o: t[:, :, o:o + 8].rearrange("p n (g h) -> p n g h", g=HG)
            gd = ga[1][:, 0:2 * NCHUNK * HEADS].rearrange("p (d n c) -> p d n c", d=2, n=NCHUNK)
            for d in range(2):
                dve.tensor_copy(kind(d, 0), lift(y, 16 + 8 * d))
                dve.tensor_copy(kind(d, 2), lift(y, 8 * d))
                gstep(dve.tensor_copy(gd[:, d, :, :], y[:, :, 16 + 8 * d:24 + 8 * d]))
            dve.sem_inc(g_lift, 1)
            dve.wait_ge(g_pe, 2)
            sums = lambda d, b: ps[:, b * HALF + 80 * d:b * HALF + 80 * d + 80].rearrange("p (n g h) -> p n g h", n=NCHUNK, g=HG)
            for d in range(2):
                gstep(dve.tensor_copy(kind(d, 1), sums(d, 1)))
                gstep(dve.tensor_copy(kind(d, 5), sums(d, 2)))
                gstep(dve.tensor_tensor(kind(d, 3), kind(d, 1), kind(d, 2), ALU.add))
                gstep(dve.tensor_tensor(kind(d, 4), kind(d, 5), kind(d, 1), ALU.subtract))
            dve.sem_inc(g_lift, 1)
            dve.wait_ge(const_loaded, 16)
            meet(dve, 4)
            for g in range(HG):
                for d in range(2):
                    dve.memset(S[g, d][:, :], 0.0).then_inc(q_["s_ready"], 1)
            dve.sem_inc(q_["qk_ready"], 2)
            dve.sem_inc(q_["o_added"], 2)
            scan(dve, scan_dve)
            meet(dve, 5)
            for h in range(HEADS):
                dve.wait_ge(r_rs, h + 1)
                need(dve, r_lo, h - 1)
                dve.tensor_tensor(rsq2[:, :], oTv[:, h, :], rrs[h % 2][:, :], ALU.mult).then_inc(r_sc, 1)
                dve.wait_ge(r_sc, h + 1)
                dve.wait_ge(r_z[h % 2], 16 * (h // 2 + 1))
                dve.scalar_tensor_tensor(rt[h % 2][:, :], rsq2[:, :], sc(C_DNW), zt[h % 2][:, :], ALU.mult, ALU.mult).then_inc(r_y, 1)
                dve.wait_ge(r_h, h + 1)
                dve.tensor_tensor(yl[:, h * LAT:(h + 1) * LAT], rt[h % 2][:, :], yh[:, h * LAT:(h + 1) * LAT].bitcast(F32),
                                  ALU.subtract).then_inc(r_lo, 1)
            meet(dve, 6)
            cut_lo(dve, Unit(U_OUT))
            for m in range(KT):
                if m + 1 < KT:
                    cut_lo(dve, Unit(U_OUT + m + 1))
                dve.wait_ge(w_used, U_OUT + m + 1)
                dve.scalar_tensor_tensor(hTv[:, m, :], bank(2 * (m % 2), 2), mod(0, 2, m, 0), hTv[:, m, :],
                                         ALU.mult, ALU.add).then_inc(r_added, 1)
                dve.wait_ge(late_loaded[m % 2], 16 * (m // 2 + 1))
                need(dve, late_used, m)
                if m == 0:
                    dve.tensor_scalar(acc0[:, :], adal[0][:, :], sc(C_SILU), None, ALU.mult).then_inc(late_used, 1)
                else:
                    dve.scalar_tensor_tensor(acc0[:, :], adal[m % 2][:, :], sc(C_SILU + 2 * m), acc0[:, :],
                                             ALU.mult, ALU.add).then_inc(late_used, 1)
            meet(dve, 7)
            late_mods(0, 24, 4)
            modulators((2,))
            dve.sem_inc(mods_done, 1)
            norm_dve(dve, "ffn0")
            dve.wait_ge(n_lo, 3 * KT + 2)
            cut_lo(dve, gu_unit(0, 0, 0, None))
            dve.memset(fpad[:, 0:1], 0.0)
            dve.memset(fpad[:, 1 + LAT:2 + LAT], 0.0)
            meet(dve, 8)
            pairs(dve, 0, up_dve(dve, fchain), fchain)
            meet(dve, 9)
            down_dve(dve, 0)
            meet(dve, 10)
            late_mods(1, 0, 6)
            modulators((3, 4))
            dve.tensor_tensor(sc(C_PG, KT), sc(C_PSCALE, KT), small_mod(1, 2, 0), ALU.mult).then_inc(mods_self, 1)
            dve.wait_ge(mods_self, 9)
            dve.sem_inc(mods_done, 1)
            norm_dve(dve, "mix1")
            meet(dve, 11)
            pool_dve(dve)
            meet(dve, 12)
            norm_dve(dve, "ffn1")
            dve.wait_ge(n_lo, 4 * KT + 2)
            cut_lo(dve, gu_unit(1, 0, 0, None))
            dve.memset(fpad[:, 0:1], 0.0)
            dve.memset(fpad[:, 1 + LAT:2 + LAT], 0.0)
            meet(dve, 13)
            pairs(dve, 1, up_dve(dve, fchain), fchain)
            meet(dve, 14)
            down_dve(dve, 1)
            meet(dve, 15)

        @block.tensor
        def _(pe):
            def late_sums(acc, n):
                for m in range(n):
                    mm = pe.matmul(ps[:, 4 * HALF + m:4 * HALF + m + 1], acc[:, m * P:(m + 1) * P], ones[:, 0:1], start=True, stop=True)
                mm.then_inc(late_summed, 1)

            pe.sem_inc(n_sum, 2)
            pe.wait_ge(start_loaded, 32)
            norm_pe(pe, "mix0")
            pe.wait_ge(ada_silu, 1)
            for i in range(KT // 2):
                pe.wait_ge(ada_loaded[i], 16)
                for k in (2 * i, 2 * i + 1):
                    for c in range(EARLY // HALF):
                        o = (k % 2) * EARLY + c * HALF
                        mm = pe.matmul(ps[0:2, (2 + c) * HALF:(3 + c) * HALF], sc(C_SILU + 2 * k, 2), adae[i][:, o:o + HALF],
                                       start=k == 0, stop=k == KT - 1)
            mm.then_inc(ada_made, 1)
            pe.wait_ge(ada_copied, 1)
            for m in range(EARLY // P):
                mm = pe.matmul(ps[:, 2 * HALF + 2 * m:2 * HALF + 2 * m + 2], mrow[:, m * P:(m + 1) * P], ident[0:2, 0:2],
                               start=True, stop=True)
            mm.then_inc(ada_turned, 1)
            norm_pe(pe, "ctx0")
            meet(pe, 1)
            meet(pe, 2)

            def slot(v):
                if v.base < U_OUT:
                    proj_pe(pe, v, kind_of(v.base))
                if U_K <= v.base - 1 < U_V:
                    proj_sums_pe(pe, v.plus(-1), kind_of(v.base - 1))
            proj_slots(pe, slot)
            meet(pe, 3)
            pe.wait_ge(const_loaded, 16)
            for n in range(NCHUNK):
                mm = pe.transpose(ps[:, n * 32:(n + 1) * 32], grow[:, n * P:(n + 1) * P], cst(K_ID)[0:32, 0:32])
            mm.then_inc(g_pe, 1)
            pe.wait_ge(g_lift, 1)
            for b, ms in ((1, (K_TRIF, K_TRIB)), (2, (K_ONES, K_ONES))):
                for d in range(2):
                    mm = pe.matmul(ps[:, b * HALF + 80 * d:b * HALF + 80 * d + 80], cst(ms[d]), ga[1][:, 80 * d:80 * d + 80],
                                   start=True, stop=True)
            mm.then_inc(g_pe, 1)
            meet(pe, 4)
            pe.sem_inc(q_["o_made"], 2)
            scan(pe, scan_pe)
            meet(pe, 5)
            for h in range(HEADS):
                pe.wait_ge(r_sq, h + 1)
                need(pe, r_rs, h - 1)
                for i in range(2):
                    mm = pe.matmul(bank(2 * (h % 2) + i), ones[:, :], rsq[h % 2][:, i * HALF:(i + 1) * HALF], start=True, stop=True)
                mm.then_inc(r_sum, 1)
            meet(pe, 6)
            for m in range(KT):
                u = Unit(U_OUT + m)
                pe.wait_ge(w_lo, u.n(1))
                need(pe, r_added, m - 1)
                outs = [(bank(2 * (m % 2) + i), (lambda i: lambda k: yh[:, k * LAT + i * HALF:k * LAT + (i + 1) * HALF])(i),
                         (lambda i: lambda k: yl[:, k * LAT + i * HALF:k * LAT + (i + 1) * HALF])(i)) for i in range(2)]
                product(pe, u, outs).then_inc(w_used, 1)
            meet(pe, 7)
            norm_pe(pe, "ffn0")
            late_sums(acc0, 24)
            meet(pe, 8)
            pairs(pe, 0, up_pe(pe))
            meet(pe, 9)
            for half in range(2):
                downs(pe, 0, half, down_pe(pe))
            meet(pe, 10)
            norm_pe(pe, "mix1")
            late_sums(acc1, 48)
            meet(pe, 11)
            pool_pe(pe)
            meet(pe, 12)
            norm_pe(pe, "ffn1")
            meet(pe, 13)
            pairs(pe, 1, up_pe(pe))
            meet(pe, 14)
            for half in range(2):
                downs(pe, 1, half, down_pe(pe))
            meet(pe, 15)


def pack_unit(w):
    return w.reshape(KT, P, P).transpose(1, 0, 2).reshape(P, UNIT)


def channels(v):
    return np.asarray(v).reshape(-1, P).T


def kernel(**inputs):
    import concourse.bacc as _bacc
    from concourse.bass_utils import run_bass_kernel_spmd as _run

    x = {k: np.asarray(v) for k, v in inputs.items()}
    w_in = x["dn_w_in"][0]
    units = [pack_unit(np.pad(w_in[:, 4 * D:], ((0, 0), (0, P - 32))))]
    for o in (D, 0, 2 * D, 3 * D):
        units += [pack_unit(w_in[:, o + P * h:o + P * (h + 1)]) for h in range(HEADS)]
    units += [pack_unit(x["dn_w_out"][0][:, P * m:P * (m + 1)]) for m in range(KT)]

    def up(L):
        out = []
        for j in range(FT):
            out += [pack_unit(x[n][L][:, P * j:P * (j + 1)]) for n in ("ffn_w_gate", "ffn_w_up")]
        return out

    def down(L):
        return [x["ffn_w_down"][L][P * k:P * (k + 1), :] for k in range(FT)]

    units += up(0) + down(0)
    pw = x["pool_w_grp"][0]
    for w in range(2):
        tiles = [pw[m // 2][P * kk:P * (kk + 1), P * (m % 2):P * (m % 2 + 1)] for m in range(4 * w, 4 * w + 4) for kk in range(2)]
        units.append(np.concatenate(tiles, axis=1))
    units += up(1) + down(1)
    w_units = np.ascontiguousarray(np.stack(units))

    edge = np.zeros((4, 2 * EDGE), np.float32)
    for i, w in enumerate(POOL_WINDOWS):
        t = np.r_[0:EDGE, LAT - EDGE:LAT]
        edge[i] = w / (np.minimum(t + w - w // 2, LAT) - np.maximum(t - w // 2, 0))
    conv = x["dn_conv"][0].reshape(TAPS, 3, KT, P)[:, [1, 0, 2]]
    rows = [
        np.stack([channels(x["c"][0]), channels(x["c_ctx"])], axis=2).reshape(P, -1),
        np.concatenate([channels(x["ada_b"][L]) for L in range(2)], axis=1),
        np.concatenate([channels(x["norm_mix_w"][L]) for L in range(2)], axis=1),
        np.concatenate([channels(x["norm_ffn_w"][L]) for L in range(2)], axis=1),
        conv.transpose(3, 1, 2, 0).reshape(P, -1),
        x["dn_norm_w"][0][:, None],
        np.concatenate([x["ffn_conv"][L].reshape(FTAPS, FT, P).transpose(2, 1, 0).reshape(P, -1) for L in range(2)], axis=1),
        np.concatenate([channels(x["ffn_conv_b"][L]) for L in range(2)], axis=1),
        channels(x["pool_scale"][0]),
        np.broadcast_to(x["dn_a_log"][0].reshape(1, 16), (P, 16)),
        np.broadcast_to(x["dn_dt_bias"][0].reshape(1, 16), (P, 16)),
        np.broadcast_to(edge.reshape(1, -1), (P, edge.size)),
        np.full((P, 1), EPS, np.float32),
    ]
    small = np.ascontiguousarray(np.concatenate(rows, axis=1))
    assert small.shape == (P, N_IN)
    arrays = {
        "xT": np.ascontiguousarray(x["x"][0].T).reshape(KT, P, LAT),
        "ctxT": np.ascontiguousarray(x["ctx"][0].T).reshape(KT, P, CTX),
        "small_in": small, "const_in": constants(), "ada_w_in": x["ada_w"], "w_units_in": w_units,
    }
    nc = _bacc.Bacc("TRN2", target_bir_lowering=False, num_devices=1)
    args = [nc.dram_tensor(n, a.shape, F32, kind="ExternalInput").ap() for n, a in arrays.items()]
    args.append(nc.dram_tensor("outT", (KT, P, LAT), F32, kind="ExternalOutput").ap())
    args += [nc.dram_tensor(n, (HEADS, P, TOK), F32, kind="Internal").ap() for n in ("k_scratch", "q_scratch", "v_scratch", "z_scratch")]
    args.append(nc.dram_tensor("h_scratch", (KT, P, LAT), F32, kind="Internal").ap())
    build(nc, *args)
    r = _run(nc, [arrays], core_ids=[0])
    got = r.results[0]["outT"]
    return np.ascontiguousarray(got.reshape(D, LAT).T)[None]
```
